# Optimizing a Trainium2 kernel written in Bass

```python
import math
import jax, jax.numpy as jnp
from jax import lax
import numpy as np

D_MODEL = 1024
BATCH = 1
SEQ = 512
DEPTH = 1

SG_WIDTH = 512
SG_GROUPS = 8
SG_GROUP_DIM = SG_WIDTH // SG_GROUPS
CHUNK = 128
CV_WIDTH = 512
CV_KERNEL = 31
SB_HEADS = 8
SB_HEAD_DIM = 64
SB_WIDTH = SB_HEADS * SB_HEAD_DIM
Q_BLOCK = 128
N_BRANCH = 3
D_FF = 2816
FFN_KERNEL = 3

IN_COLS = 2 * SG_WIDTH + 2 * CV_WIDTH + 3 * SB_WIDTH + N_BRANCH * D_MODEL
EPS = 1e-6


def rms_norm(x, g):
    xf = x.astype(jnp.float32)
    y = xf * lax.rsqrt(jnp.mean(xf * xf, axis=-1, keepdims=True) + EPS)
    return (y * g.astype(jnp.float32)).astype(x.dtype)

def layer_norm(x, g, b):
    xf = x.astype(jnp.float32)
    mu = jnp.mean(xf, axis=-1, keepdims=True)
    xc = xf - mu
    y = xc * lax.rsqrt(jnp.mean(xc * xc, axis=-1, keepdims=True) + EPS)
    return (y * g.astype(jnp.float32) + b.astype(jnp.float32)).astype(x.dtype)

def causal_depthwise_conv(x, w, b):
    k_width, ch = w.shape
    y = lax.conv_general_dilated(
        x, w[:, None, :].astype(x.dtype), window_strides=(1,), padding=[(k_width - 1, 0)],
        dimension_numbers=("NWC", "WIO", "NWC"), feature_group_count=ch)
    return y + b.astype(x.dtype)

def chunked_spatial_gating(v, w_s, b_s):
    bsz, t, _ = v.shape
    vc = v.reshape(bsz, t // CHUNK, CHUNK, SG_GROUPS, SG_GROUP_DIM)
    tril = jnp.tril(jnp.ones((CHUNK, CHUNK), dtype=bool))
    w_m = jnp.where(tril[None], w_s, jnp.zeros_like(w_s)).astype(v.dtype)
    out = jnp.einsum("gts,bcsgd->bctgd", w_m, vc) + b_s.T.astype(v.dtype)[:, :, None]
    return out.reshape(bsz, t, SG_WIDTH)

def stick_breaking_attention(q, k, v):
    bsz, t, h, dh = q.shape
    q = q.transpose(0, 2, 1, 3)
    k = k.transpose(0, 2, 1, 3)
    v = v.transpose(0, 2, 1, 3)
    scale = 1.0 / math.sqrt(dh)
    outs = []
    for i in range(t // Q_BLOCK):
        ctx = (i + 1) * Q_BLOCK
        q_blk = q[:, :, i * Q_BLOCK:ctx]
        z = jnp.einsum("bhqd,bhkd->bhqk", q_blk, k[:, :, :ctx]).astype(jnp.float32) * scale
        q_pos = i * Q_BLOCK + jnp.arange(Q_BLOCK)
        k_pos = jnp.arange(ctx)
        mask = k_pos[None, :] < q_pos[:, None]
        log_1m_beta = jnp.where(mask, jax.nn.log_sigmoid(-z), 0.0)
        cs = lax.cumsum(log_1m_beta, axis=3)
        log_a = jax.nn.log_sigmoid(z) + (cs[..., -1:] - cs)
        a = jnp.where(mask, jnp.exp(log_a), 0.0)
        outs.append(jnp.einsum("bhqk,bhkd->bhqd", a.astype(v.dtype), v[:, :, :ctx]))
    o = jnp.concatenate(outs, axis=2)
    return o.transpose(0, 2, 1, 3).reshape(bsz, t, h * dh)

def first_inputs(seed: int = 0) -> dict:
    key = jax.random.key(seed)
    ks = jax.random.split(key, 24)
    f32 = jnp.float32
    L, D = DEPTH, D_MODEL

    def nrm(k, shape, scale):
        return jax.random.normal(k, shape, f32) * scale

    return {
        "x": jax.random.normal(ks[0], (BATCH, SEQ, D), f32),
        "ln1_g": 1.0 + nrm(ks[1], (L, D), 0.05),
        "w_in": nrm(ks[2], (L, D, IN_COLS), D ** -0.5),
        "b_gate": nrm(ks[3], (L, N_BRANCH, D), 0.1),
        "sg_ln_g": 1.0 + nrm(ks[4], (L, SG_WIDTH), 0.05),
        "sg_ln_b": nrm(ks[5], (L, SG_WIDTH), 0.05),
        "sg_w": nrm(ks[6], (L, SG_GROUPS, CHUNK, CHUNK), CHUNK ** -0.5),
        "sg_b": 1.0 + nrm(ks[7], (L, SG_GROUPS, CHUNK), 0.1),
        "w_a_out": nrm(ks[8], (L, SG_WIDTH, D), SG_WIDTH ** -0.5),
        "cv_w": nrm(ks[9], (L, CV_KERNEL, CV_WIDTH), CV_KERNEL ** -0.5),
        "cv_b": nrm(ks[10], (L, CV_WIDTH), 0.05),
        "cv_ln_g": 1.0 + nrm(ks[11], (L, CV_WIDTH), 0.05),
        "cv_ln_b": nrm(ks[12], (L, CV_WIDTH), 0.05),
        "w_b_out": nrm(ks[13], (L, CV_WIDTH, D), CV_WIDTH ** -0.5),
        "q_norm_g": 1.0 + nrm(ks[14], (L, SB_HEAD_DIM), 0.05),
        "k_norm_g": 1.0 + nrm(ks[15], (L, SB_HEAD_DIM), 0.05),
        "w_c_out": nrm(ks[16], (L, SB_WIDTH, D), SB_WIDTH ** -0.5),
        "w_out": nrm(ks[17], (L, D, D), D ** -0.5),
        "ln2_g": 1.0 + nrm(ks[18], (L, D), 0.05),
        "w_up": nrm(ks[19], (L, D, 2 * D_FF), D ** -0.5),
        "ffn_conv_w": nrm(ks[20], (L, FFN_KERNEL, 2 * D_FF), FFN_KERNEL ** -0.5),
        "ffn_conv_b": nrm(ks[21], (L, 2 * D_FF), 0.05),
        "w_down": nrm(ks[22], (L, D_FF, D), D_FF ** -0.5),
    }

def first_block(x, ln1_g, w_in, b_gate, sg_ln_g, sg_ln_b, sg_w, sg_b, w_a_out,
              cv_w, cv_b, cv_ln_g, cv_ln_b, w_b_out, q_norm_g, k_norm_g, w_c_out,
              w_out, ln2_g, w_up, ffn_conv_w, ffn_conv_b, w_down):
    bsz, t, d = x.shape
    split_at = np.cumsum([2 * SG_WIDTH, 2 * CV_WIDTH, 3 * SB_WIDTH]).tolist()
    for l in range(DEPTH):
        h = rms_norm(x, ln1_g[l])
        z = h @ w_in[l]
        z_a, z_b, z_c, z_g = jnp.split(z, split_at, axis=-1)

        a = jax.nn.gelu(z_a)
        u, v = jnp.split(a, 2, axis=-1)
        v = layer_norm(v, sg_ln_g[l], sg_ln_b[l])
        y_a = (u * chunked_spatial_gating(v, sg_w[l], sg_b[l])) @ w_a_out[l]

        p, g_lin = jnp.split(z_b, 2, axis=-1)
        c = p * jax.nn.sigmoid(g_lin)
        c = causal_depthwise_conv(c, cv_w[l], cv_b[l])
        c = jax.nn.silu(layer_norm(c, cv_ln_g[l], cv_ln_b[l]))
        y_b = c @ w_b_out[l]

        q, k, vv = jnp.split(z_c, 3, axis=-1)
        q = rms_norm(q.reshape(bsz, t, SB_HEADS, SB_HEAD_DIM), q_norm_g[l])
        k = rms_norm(k.reshape(bsz, t, SB_HEADS, SB_HEAD_DIM), k_norm_g[l])
        vv = vv.reshape(bsz, t, SB_HEADS, SB_HEAD_DIM)
        y_c = stick_breaking_attention(q, k, vv) @ w_c_out[l]

        gates = jax.nn.sigmoid(z_g.reshape(bsz, t, N_BRANCH, d) + b_gate[l].astype(z_g.dtype))
        merged = gates[:, :, 0] * y_a + gates[:, :, 1] * y_b + gates[:, :, 2] * y_c
        x = x + merged @ w_out[l]

        h2 = rms_norm(x, ln2_g[l])
        up = causal_depthwise_conv(h2 @ w_up[l], ffn_conv_w[l], ffn_conv_b[l])
        gate, val = jnp.split(up, 2, axis=-1)
        x = x + (jax.nn.silu(gate) * val) @ w_down[l]
    return x


D_RNN = 1024
N_RNN_BLOCKS = 8
RNN_BLOCK = D_RNN // N_RNN_BLOCKS
CONV_WIDTH = 4
LRU_C = 8.0
HEAD_DIM = 64
N_Q_HEADS = 16
N_KV_HEADS = 4
Q_PER_KV = N_Q_HEADS // N_KV_HEADS
D_ATTN = N_Q_HEADS * HEAD_DIM
D_KV = N_KV_HEADS * HEAD_DIM
WINDOW = 128
BLOCK = 128
ROPE_DIM = HEAD_DIM // 4
ROPE_THETA = 500000.0
NORM_EPS = 1e-6

OFF_RNN_X = 0
OFF_RNN_G = OFF_RNN_X + D_RNN
OFF_Q = OFF_RNN_G + D_RNN
OFF_K = OFF_Q + D_ATTN
OFF_V = OFF_K + D_KV
OFF_ATTN_G = OFF_V + D_KV
OFF_MERGE_R = OFF_ATTN_G + D_ATTN
OFF_MERGE_A = OFF_MERGE_R + D_MODEL
D_IN = OFF_MERGE_A + D_MODEL


def rms_norm_2(x, g):
    xf = x.astype(jnp.float32)
    y = xf * lax.rsqrt(jnp.mean(xf * xf, axis=-1, keepdims=True) + NORM_EPS)
    return (y * g.astype(jnp.float32)).astype(x.dtype)

def causal_depthwise_conv_2(u, w, b):
    C = u.shape[-1]
    y = lax.conv_general_dilated(
        u, w.astype(u.dtype)[:, None, :], window_strides=(1,),
        padding=[(CONV_WIDTH - 1, 0)], dimension_numbers=("NWC", "WIO", "NWC"),
        feature_group_count=C)
    return y + b.astype(u.dtype)

def block_diag_linear(u, w, b):
    B, S, _ = u.shape
    ub = u.reshape(B, S, N_RNN_BLOCKS, RNN_BLOCK)
    y = jnp.einsum("bsnc,ncd->bsnd", ub, w.astype(u.dtype))
    return y.reshape(B, S, D_RNN) + b.astype(u.dtype)

def rg_lru(u, w_a, b_a, w_x, b_x, lam):
    r = jax.nn.sigmoid(block_diag_linear(u, w_a, b_a).astype(jnp.float32))
    i = jax.nn.sigmoid(block_diag_linear(u, w_x, b_x).astype(jnp.float32))
    log_a = -LRU_C * r * jax.nn.softplus(-lam.astype(jnp.float32))
    a = jnp.exp(log_a)
    b = jnp.sqrt(-jnp.expm1(2.0 * log_a)) * (i * u.astype(jnp.float32))

    def combine(c1, c2):
        a1, b1 = c1
        a2, b2 = c2
        return a1 * a2, a2 * b1 + b2

    _, h = lax.associative_scan(combine, (a, b), axis=1)
    return h.astype(u.dtype)

def rope_tables(seq_len):
    pos = jnp.arange(seq_len, dtype=jnp.float32)
    inv_freq = ROPE_THETA ** (-jnp.arange(0, ROPE_DIM, 2, dtype=jnp.float32) / ROPE_DIM)
    ang = pos[:, None] * inv_freq[None, :]
    return jnp.cos(ang)[:, None, :], jnp.sin(ang)[:, None, :]

def apply_partial_rope(t, cos, sin):
    half = ROPE_DIM // 2
    c = cos.astype(t.dtype)
    s = sin.astype(t.dtype)
    t1 = t[..., :half]
    t2 = t[..., half:ROPE_DIM]
    rot = jnp.concatenate([t1 * c - t2 * s, t2 * c + t1 * s], axis=-1)
    return jnp.concatenate([rot, t[..., ROPE_DIM:]], axis=-1)

def sliding_window_attention_with_sinks(q, k, v, sinks):
    B, S, _, _ = q.shape
    nb = S // BLOCK
    qb = q.reshape(B, nb, BLOCK, N_KV_HEADS, Q_PER_KV, HEAD_DIM)
    kb = k.reshape(B, nb, BLOCK, N_KV_HEADS, HEAD_DIM)
    vb = v.reshape(B, nb, BLOCK, N_KV_HEADS, HEAD_DIM)
    zeros = jnp.zeros_like(kb[:, :1])
    kw = jnp.concatenate([jnp.concatenate([zeros, kb[:, :-1]], axis=1), kb], axis=2)
    vw = jnp.concatenate([jnp.concatenate([zeros, vb[:, :-1]], axis=1), vb], axis=2)

    scale = 1.0 / math.sqrt(HEAD_DIM)
    scores = jnp.einsum("bnqkgd,bnjkd->bnkgqj", qb, kw).astype(jnp.float32) * scale

    blk = jnp.arange(nb)[:, None, None]
    q_abs = blk * BLOCK + jnp.arange(BLOCK)[None, :, None]
    k_abs = (blk - 1) * BLOCK + jnp.arange(2 * BLOCK)[None, None, :]
    valid = (k_abs <= q_abs) & (q_abs - k_abs < WINDOW) & (k_abs >= 0)
    scores = jnp.where(valid[None, :, None, None, :, :], scores, -jnp.inf)

    sink = sinks.astype(jnp.float32).reshape(N_KV_HEADS, Q_PER_KV)[None, None, :, :, None]
    m = jnp.maximum(jnp.max(scores, axis=-1), sink)
    p = jnp.exp(scores - m[..., None])
    denom = jnp.sum(p, axis=-1) + jnp.exp(sink - m)
    probs = (p / denom[..., None]).astype(v.dtype)
    out = jnp.einsum("bnkgqj,bnjkd->bnqkgd", probs, vw)
    return out.reshape(B, S, D_ATTN)

def second_inputs(seed: int = 0) -> dict:
    key = jax.random.key(seed)
    ks = jax.random.split(key, 17)
    f32 = jnp.float32
    x = jax.random.normal(ks[0], (BATCH, SEQ, D_MODEL), f32)
    norm_g = 1.0 + 0.02 * jax.random.normal(ks[1], (DEPTH, D_MODEL), f32)
    w_in = jax.random.normal(ks[2], (DEPTH, D_MODEL, D_IN), f32) * D_MODEL ** -0.5
    conv_w = jax.random.normal(ks[3], (DEPTH, CONV_WIDTH, D_RNN), f32) * CONV_WIDTH ** -0.5
    conv_b = 0.02 * jax.random.normal(ks[4], (DEPTH, D_RNN), f32)
    lru_w_a = jax.random.normal(ks[5], (DEPTH, N_RNN_BLOCKS, RNN_BLOCK, RNN_BLOCK), f32) * RNN_BLOCK ** -0.5
    lru_b_a = 0.02 * jax.random.normal(ks[6], (DEPTH, D_RNN), f32)
    lru_w_x = jax.random.normal(ks[7], (DEPTH, N_RNN_BLOCKS, RNN_BLOCK, RNN_BLOCK), f32) * RNN_BLOCK ** -0.5
    lru_b_x = 0.02 * jax.random.normal(ks[8], (DEPTH, D_RNN), f32)
    a0 = jax.random.uniform(ks[9], (DEPTH, D_RNN), f32, 0.9, 0.999)
    lru_lambda = jnp.log(a0) - jnp.log1p(-a0)
    attn_sinks = 0.5 * jax.random.normal(ks[10], (DEPTH, N_Q_HEADS), f32)
    w_rnn_out = jax.random.normal(ks[11], (DEPTH, D_RNN, D_MODEL), f32) * D_RNN ** -0.5
    w_attn_out = jax.random.normal(ks[12], (DEPTH, D_ATTN, D_MODEL), f32) * D_ATTN ** -0.5
    w_o = jax.random.normal(ks[13], (DEPTH, D_MODEL, D_MODEL), f32) * D_MODEL ** -0.5
    final_norm_g = 1.0 + 0.02 * jax.random.normal(ks[14], (D_MODEL,), f32)
    return {"x": x, "norm_g": norm_g, "w_in": w_in, "conv_w": conv_w, "conv_b": conv_b,
            "lru_w_a": lru_w_a, "lru_b_a": lru_b_a, "lru_w_x": lru_w_x, "lru_b_x": lru_b_x,
            "lru_lambda": lru_lambda, "attn_sinks": attn_sinks, "w_rnn_out": w_rnn_out,
            "w_attn_out": w_attn_out, "w_o": w_o, "final_norm_g": final_norm_g}

def second_block(x, norm_g, w_in, conv_w, conv_b, lru_w_a, lru_b_a, lru_w_x, lru_b_x,
              lru_lambda, attn_sinks, w_rnn_out, w_attn_out, w_o, final_norm_g):
    B, S, _ = x.shape
    cos, sin = rope_tables(S)
    for l in range(DEPTH):
        h = rms_norm_2(x, norm_g[l])
        proj = jnp.einsum("bsd,de->bse", h, w_in[l])
        u = proj[..., OFF_RNN_X:OFF_RNN_G]
        g_rnn = proj[..., OFF_RNN_G:OFF_Q]
        q = proj[..., OFF_Q:OFF_K].reshape(B, S, N_Q_HEADS, HEAD_DIM)
        k = proj[..., OFF_K:OFF_V].reshape(B, S, N_KV_HEADS, HEAD_DIM)
        v = proj[..., OFF_V:OFF_ATTN_G].reshape(B, S, N_KV_HEADS, HEAD_DIM)
        g_attn = proj[..., OFF_ATTN_G:OFF_MERGE_R]
        m_rnn = proj[..., OFF_MERGE_R:OFF_MERGE_A]
        m_attn = proj[..., OFF_MERGE_A:D_IN]

        u = causal_depthwise_conv_2(u, conv_w[l], conv_b[l])
        y_rnn = rg_lru(u, lru_w_a[l], lru_b_a[l], lru_w_x[l], lru_b_x[l], lru_lambda[l]) * jax.nn.silu(g_rnn)

        q = apply_partial_rope(q, cos, sin)
        k = apply_partial_rope(k, cos, sin)
        y_attn = sliding_window_attention_with_sinks(q, k, v, attn_sinks[l]) * jax.nn.silu(g_attn)

        merged = (jax.nn.sigmoid(m_rnn) * jnp.einsum("bsr,rd->bsd", y_rnn, w_rnn_out[l])
                  + jax.nn.sigmoid(m_attn) * jnp.einsum("bsa,ad->bsd", y_attn, w_attn_out[l]))
        x = x + jnp.einsum("bsd,de->bse", merged, w_o[l])
    return rms_norm_2(x, final_norm_g)


def setup_inputs(seed=0):
    out = dict(first_inputs(seed))
    for name, value in second_inputs(seed + 1).items():
        if name != "x":
            out[name + "_2"] = value
    return out


def reference(
    x, ln1_g, w_in, b_gate, sg_ln_g, sg_ln_b, sg_w, sg_b, w_a_out, cv_w, cv_b, cv_ln_g, cv_ln_b,
    w_b_out, q_norm_g, k_norm_g, w_c_out, w_out, ln2_g, w_up, ffn_conv_w, ffn_conv_b, w_down,
    norm_g_2, w_in_2, conv_w_2, conv_b_2, lru_w_a_2, lru_b_a_2, lru_w_x_2, lru_b_x_2,
    lru_lambda_2, attn_sinks_2, w_rnn_out_2, w_attn_out_2, w_o_2, final_norm_g_2,
):
    x = first_block(
        x, ln1_g, w_in, b_gate, sg_ln_g, sg_ln_b, sg_w, sg_b, w_a_out, cv_w, cv_b, cv_ln_g,
        cv_ln_b, w_b_out, q_norm_g, k_norm_g, w_c_out, w_out, ln2_g, w_up, ffn_conv_w,
        ffn_conv_b, w_down,
    )
    return second_block(
        x, norm_g_2, w_in_2, conv_w_2, conv_b_2, lru_w_a_2, lru_b_a_2, lru_w_x_2, lru_b_x_2,
        lru_lambda_2, attn_sinks_2, w_rnn_out_2, w_attn_out_2, w_o_2, final_norm_g_2,
    )


_drawn_inputs = setup_inputs


def setup_inputs(seed=0):
    import zlib

    import numpy as np

    out = dict(_drawn_inputs(seed))
    spreads = {}
    factors = {'sg_ln_g': 4.952,
     'sg_ln_b': 4.713,
     'cv_ln_g': 2.93,
     'cv_ln_b': 3.515,
     'q_norm_g': 7.554,
     'k_norm_g': 7.9,
     'norm_g_2': 8.0,
     'conv_b_2': 5.558,
     'lru_b_a_2': 42.343,
     'lru_b_x_2': 35.286,
     'attn_sinks_2': 38.72,
     'final_norm_g_2': 8.086}
    for name, (base, spread) in spreads.items():
        noise = np.random.default_rng([zlib.crc32(name.encode()), seed]).standard_normal(out[name].shape)
        drawn = base * np.exp(spread * noise) if base else spread * noise
        out[name] = __import__('jax').numpy.asarray(drawn.astype(out[name].dtype))
    for name, factor in factors.items():
        out[name] = (out[name] * factor).astype(out[name].dtype)
    return out
```

```python
import math
from contextlib import ExitStack

import concourse.bass as bass
from concourse import mybir

F32 = mybir.dt.float32
F32R = mybir.dt.float32r
ALU = mybir.AluOpType
ACT = mybir.ActivationFunctionType
AX = mybir.AxisListType

P = 128
SEQ = 512
TT = SEQ // P
D = 1024
KD = D // P
W = 512
KW = W // P
CHUNK = 128
CVK = 31
HEADS = 8
DH = 64
D_FF = 2816
NF = D_FF // P
FFK = 3
EPS = 1e-6
BIG = 1e30

RNN_TAPS = 4
KVH = 4
QPK = 4
ROPE_DIM = 16
ROPE_HALF = ROPE_DIM // 2
ROPE_THETA = 500000.0
LRU_C = 8.0

IN_U, IN_VSG, IN_P, IN_G, IN_Q, IN_K, IN_V, IN_GATE = (i * W for i in range(8))
IN2_U, IN2_G, IN2_Q, IN2_KV, IN2_GA, IN2_MR, IN2_MA = 0, 1024, 2048, 3072, 3584, 4608, 5632

U_A = 0
U_B = U_A + 16
U_C = U_B + 12
U_D = U_C + 36
U_E = U_D + 8
U_F = U_E + 2 * NF
U_G = U_F + NF
U_GA = U_G + 12
U_GR = U_GA + 8
U_H = U_GR + 16
U_O = U_H + 32
U_END = U_O + 8

BRANCHES = (0, 2, 1)

DR_A = KD
DR_B = DR_A + 16
DR_C = DR_B + 12
DR_D = DR_C + 48
DR_E = DR_D + KD
DR_F = DR_E + 2 * NF
DR_G = DR_F + KD
DR_GA = DR_G + 12
DR_GR = DR_GA + 8
DR_H = DR_GR + 16
DR_O = DR_H + 32

V_CVW = 0
V_QKG = V_CVW + CVK * KW
V_FW = [128, 128 + NF * 2, 256]
V_CW2 = V_FW[1] + NF * 2
V_LN1 = V_CW2 + RNN_TAPS * KD
V_FB = V_FW[2] + NF * 2
V_BG = V_FB + NF * 2
V_LN2 = V_BG + 3 * KD
V_NG2 = V_LN2 + KD
V_CVB = 384
V_CLG = V_CVB + KW
V_CLB = V_CLG + KW
V_CB2 = V_CLB + KW
V_BA = V_CB2 + KD
V_BX = V_BA + KD
V_LAM = V_BX + KD
V_END = V_LAM + KD
assert V_LN1 + KD == 256 and V_NG2 + KD == 384

S_RTOK = 0
S_SP8 = 4
S_QKS = 16
S_LN = 80
S_ATT = 140
S_FIN = 200
S_NSP8 = 220
N_VEC = 21


def unit_kind(n):
    if n < U_B or U_G <= n < U_GA or n >= U_O:
        return "T"
    if U_C <= n < U_D:
        return "M" if (n - U_C) % 6 < 4 else "T"
    if U_F <= n < U_G:
        return "F"
    return "M"


def program(nc, x, ln1_g, w_in, b_gate, sg_ln_g, sg_ln_b, sg_w, sg_b, w_a_out, cv_w, cv_b, cv_ln_g,
            cv_ln_b, w_b_out, q_norm_g, k_norm_g, w_c_out, w_out, ln2_g, w_up, ffn_conv_w,
            ffn_conv_b, w_down, norm_g_2, w_in_2, conv_w_2, conv_b_2, lru_w_a_2, lru_b_a_2,
            lru_w_x_2, lru_b_x_2, lru_lambda_2, attn_sinks_2, w_rnn_out_2, w_attn_out_2, w_o_2,
            final_norm_g_2, rope, out):
    base = (nc.sbuf_base + 31) // 32 * 32

    def at(name, shape, dt, kb):
        size = 4 * math.prod(shape[1:])
        assert base + int(kb * 1024) + size <= 229344, name
        return nc.alloc_sbuf_tensor_at(name, shape, dt, offset=base + int(kb * 1024))

    with ExitStack() as ctx:
        STAGE = at("STAGE", [P, 2, 2048], F32, 0)
        WH = at("WH", [P, 4, 1024], F32R, 16)
        WL = at("WL", [P, 4, 1024], F32R, 32)
        XH = at("XH", [P, KD, SEQ], F32R, 48)
        XL = at("XL", [P, KD, SEQ], F32R, 64)
        IDENT = at("IDENT", [P, P], F32, 80)
        NTRI = at("NTRI", [P, P], F32, 80.5)
        NONE_ = at("NONES", [P, P], F32, 81)
        ONES = at("ONES", [P, P], F32, 81.5)
        MSTR = at("MSTR", [P, 2, P], F32, 82)
        MMIN = at("MMIN", [P, 2, P], F32, 83)
        VEC = at("VEC", [P, 512], F32, 84)
        RBC = at("RBC", [P, SEQ], F32, 86)
        SGB = at("SGB", [P, KW, P], F32, 88)
        SMALL = at("SMALL", [P, 256], F32, 90)
        SS = at("SS", [P, SEQ], F32, 91)
        SQ = at("SQ", [P, SEQ], F32, 93)
        MINC = at("MINC", [P, P], F32, 95)
        SINK = at("SINK", [P, 16], F32, 95.5)
        ROPE = at("ROPE", [P, TT, 16], F32, 95.5625)
        XTOK = at("XTOK", [P, TT, D], F32, 96)
        QK = at("QK", [P, 2, TT, W], F32, 96)
        MERG = at("MERG", [P, KD, SEQ], F32, 96)
        XCM = at("XCM", [P, KD, SEQ], F32, 112)
        QKT = at("QKT", [P, 2, KW, SEQ], F32, 112)
        VATT = at("VATT", [P, TT, W], F32, 128)
        VSG = at("VSG", [P, TT, W], F32, 136)
        TG1 = at("TG1", [P, SEQ], F32, 144)
        CPAD = at("CPAD", [P, KW, 544], F32, 146)
        CACC = at("CACC", [P, KW, SEQ], F32, 155)
        UU = at("UU", [P, KW, SEQ], F32, 163)
        ATT = at("ATT", [P, KW, SEQ], F32, 171)
        SGLN = at("SGLN", [P, 2, W], F32, 171)
        ABUF = at("ABUF", [P, 1280], F32, 179)
        WT = at("WT", [P, 8, P], F32, 184)
        SGW = at("SGW", [P, 8, P], F32, 188)
        BH = at("BH", [P, KW, SEQ], F32R, 179)
        BL = at("BL", [P, KW, SEQ], F32R, 187)
        ROWS = at("ROWS", [P, 4, P], F32, 195)
        E1 = at("E1", [P, 1280], F32, 195)
        SPB = at("SPB", [P, 1280], F32, 200)
        TG0 = at("TG0", [P, SEQ], F32, 205)
        GS = at("GS", [P, 4, SEQ], F32, 195)
        TMPY = at("TMPY", [P, SEQ], F32, 203)
        X1 = at("X1", [P, KD, SEQ], F32, 112)
        MH = at("MH", [P, KD, SEQ], F32R, 128)
        ML = at("ML", [P, KD, SEQ], F32R, 144)
        GF = at("GF", [P, NF, SEQ], F32, 128)
        FH = at("FH", [P, 2, 2, SEQ], F32R, 172)
        FL = at("FL", [P, 2, 2, SEQ], F32R, 180)
        UPB = at("UPB", [P, 4, 516], F32, 188)
        YB = at("YB", [P, 4, SEQ], F32, 197)
        YA = at("YA", [P, KD, SEQ], F32, 96)
        Q2 = at("Q2", [P, TT, D], F32, 128)
        YR = at("YR", [P, KD, SEQ], F32, 128)
        KDUP = at("KDUP", [P, TT, KVH, 2 * DH], F32, 144)
        LRUW = at("LRUW", [P, 2 * KD, P], F32, 144)
        V2 = at("V2", [P, TT, 256], F32, 152)
        Q2T = at("Q2T", [P, KD, SEQ], F32, 156)
        K2T = at("K2T", [P, KVH, P + SEQ], F32, 172)
        AM = at("AM", [P, 3, P], F32, 182)
        S2 = [at("S2A", [P, 2, 2, 256], F32, 183.5), None]
        PT = at("PT", [P, 2, 2, 2, P], F32, 187.5)
        UP2 = at("UP2", [P, 2, 516], F32, 191.5)
        RT = at("RT", [P, 4, SEQ], F32, 196)
        S2[1] = at("S2B", [P, 2, 2, 256], F32, 195.625)
        RR = [at(f"RR{i}", [P, SEQ], F32, 199.625 + 2 * i) for i in range(2)]
        II = [at(f"II{i}", [P, SEQ], F32, 203.625 + 2 * i) for i in range(2)]
        UC = [at("UC0", [P, SEQ], F32, 80.5), at("UC1", [P, SEQ], F32, 88)]
        GT = at("GT", [P, 2, SEQ], F32, 91)
        BH2 = at("BH2", [P, KD, SEQ], F32R, 156)
        BL2 = at("BL2", [P, KD, SEQ], F32R, 172)
        MERG2 = at("MERG2", [P, KD, SEQ], F32, 128)
        GS2 = at("GS2", [P, 2, SEQ], F32, 144)
        FG = at("FG", [P, D], F32, 148)
        TMP2 = at("TMP2", [P, SEQ], F32, 152)
        M2H = at("M2H", [P, KD, SEQ], F32R, 96)
        M2L = at("M2L", [P, KD, SEQ], F32R, 188)
        XT2 = at("XT2", [P, TT, D], F32, 48)
        SQF = at("SQF", [P, D], F32, 64)

        PS = ctx.enter_context(nc.psum_tensor("PS", [P, 8, 512], F32))
        XSCR = nc.dram_tensor("x_channel_major", [P, KD * SEQ], F32, kind="Internal").ap()

        def sem(name):
            return ctx.enter_context(nc.semaphore(name))

        landed = [sem("landed0"), sem("landed1")]
        x_in = [sem(f"x_in{t}") for t in range(TT)]
        vec_in, bc_in, sgw_in = sem("vec_in"), sem("bc_in"), sem("sgw_in")
        xscr_out, xres_in = sem("xscr_out"), sem("xres_in")
        lruw_in, fg_in, stored = sem("lruw_in"), sem("fg_in"), sem("stored")
        consts = sem("consts")
        ss_added = sem("ss_added")
        ss_clear = sem("ss_clear")
        hi_done, lo_done = sem("hi_done"), sem("lo_done")
        unit_done = sem("unit_done")
        drained = sem("drained")
        xt_done = sem("xt_done")
        vec_t, vec_ready = sem("vec_t"), sem("vec_ready")
        wt_t, wt_ready = sem("wt_t"), sem("wt_ready")
        xh_ready, xl_ready, sq_ready = sem("xh_ready"), sem("xl_ready"), sem("sq_ready")
        stat_done, ms_ready, rt_ready, r_ready = (sem("stat_done"), sem("ms_ready"),
                                                  sem("rt_ready"), sem("r_ready"))
        qk_sq, qk_red, qk_ms, qk_rt, qk_ready = (sem("qk_sq"), sem("qk_red"), sem("qk_ms"),
                                                 sem("qk_rt"), sem("qk_ready"))
        qkt_t, qkt_ready = sem("qkt_t"), sem("qkt_ready")
        vg_ready, vg_var, vg_sd, vn_ready = (sem("vg_ready"), sem("vg_var"), sem("vg_sd"),
                                             sem("vn_ready"))
        sg_done, sg_read = sem("sg_done"), sem("sg_read")
        sc_done, ln_ready, sp_ready, tri_done = (sem("sc_done"), sem("ln_ready"), sem("sp_ready"),
                                                 sem("tri_done"))
        min_ready, a_ready, av_done, att_read = (sem("min_ready"), sem("a_ready"), sem("av_done"),
                                                 sem("att_read"))
        tg_act, tg_used = sem("tg_act"), sem("tg_used")
        c_sum, c_mean, c_cent, c_sq, c_ssum, c_var, c_ve, c_sd, c_norm, c_ready = (
            sem("c_sum"), sem("c_mean"), sem("c_cent"), sem("c_sq"), sem("c_ssum"), sem("c_var"),
            sem("c_ve"), sem("c_sd"), sem("c_norm"), sem("c_ready"))
        bh_ready, bl_ready = sem("bh_ready"), sem("bl_ready")
        gs_ready, merged = sem("gs_ready"), sem("merged")
        mh_ready, ml_ready = sem("mh_ready"), sem("ml_ready")
        y_first, y_silu, gf_ready = sem("y_first"), sem("y_silu"), sem("gf_ready")
        y_conv = sem("y_conv")
        fh_ready, fl_ready = sem("fh_ready"), sem("fl_ready")
        rope_ready, rt_t, q2t_ready = sem("rope_ready"), sem("rt_t"), sem("q2t_ready")
        ya_silu = sem("ya_silu")
        uc_first, uc_ready, bd_done = sem("uc_first"), sem("uc_ready"), sem("bd_done")
        gate_ri, tanh_ready, a_exp = sem("gate_ri"), sem("tanh_ready"), sem("a_exp")
        bsq_ready, bsqrt, iu_ready, h_ready = (sem("bsq_ready"), sem("bsqrt"), sem("iu_ready"),
                                               sem("h_ready"))
        yr_ready, yg_sig, yg_ready = sem("yr_ready"), sem("yg_sig"), sem("yg_ready")
        s2_mask, qk2_done, s2_max, s2_exp, s2_ready, pt_t, pt_ready, pv_done, pv_read = (
            sem("s2_mask"), sem("qk2_done"), sem("s2_max"), sem("s2_exp"), sem("s2_ready"),
            sem("pt_t"), sem("pt_ready"), sem("pv_done"), sem("pv_read"))
        c_tap, y_tap = sem("c_tap"), sem("y_tap")
        bh2_ready, bl2_ready, gs2_ready, merged2 = (sem("bh2_ready"), sem("bl2_ready"),
                                                    sem("gs2_ready"), sem("merged2"))
        m2h_ready, m2l_ready = sem("m2h_ready"), sem("m2l_ready")
        x2t_t, x2t_ready, fin_sq, fin_ms, fin_sd, fin_ready = (
            sem("x2t_t"), sem("x2t_ready"), sem("fin_sq"), sem("fin_ms"), sem("fin_sd"),
            sem("fin_ready"))
        vchain, schain, gchain = sem("vchain"), sem("schain"), sem("gchain")

        def staged(n):
            kind, st, u = unit_kind(n), STAGE[:, n // 2 % 2, :], n % 2
            if kind == "M":
                return st.rearrange("p (k c) -> p k c", k=8)[:, :, u * P:(u + 1) * P]
            if kind == "T":
                return st[:, u * 1024:(u + 1) * 1024].rearrange("p (k c) -> p k c", k=2)
            return st.rearrange("p (k c) -> p k c", k=2)[:, :, u * 512:(u + 1) * 512]

        def ring(buf, n):
            k = 8 if unit_kind(n) == "M" else 2
            return buf[:, n % 4, :].rearrange("p (k c) -> p k c", k=k)

        def col(c, n=1):
            return VEC[:, c:c + n]

        def rows(w, r0, nr, c0, ncol):
            return w[0, r0 * P:(r0 + nr) * P, c0:c0 + ncol].rearrange("(k p) c -> p k c", p=P)

        def transfers():
            for c0 in (IN_Q, IN_K, IN_VSG, IN_V):
                for r0 in (0, 4):
                    yield rows(w_in, r0, 4, c0, 512)
            for c0 in (IN_P, IN_G, IN_P + 256, IN_G + 256, IN_U, IN_U + 256):
                yield rows(w_in, 0, 8, c0, 256)
            for b in BRANCHES:
                for quad in range(2):
                    for h in range(2):
                        yield rows(w_in, 0, 8, IN_GATE + b * D + quad * 512 + h * 256, 256)
                    yield rows((w_a_out, w_b_out, w_c_out)[b], 0, 4, quad * 512, 512)
            for m in range(4):
                yield rows(w_out, 0, 8, m * 256, 256)
            for f in range(NF // 2):
                yield rows(w_up, 0, 8, f * 256, 256)
                yield rows(w_up, 0, 8, D_FF + f * 256, 256)
            for kk in range(NF // 2):
                yield rows(w_down, 2 * kk, 2, 0, 1024)
            for c0 in (IN2_Q, IN2_Q + 512, IN2_KV):
                for r0 in (0, 4):
                    yield rows(w_in_2, r0, 4, c0, 512)
            for m in range(4):
                yield rows(w_in_2, 0, 8, IN2_GA + m * 256, 256)
            for m in range(4):
                yield rows(w_in_2, 0, 8, IN2_U + m * 256, 256)
                yield rows(w_in_2, 0, 8, IN2_G + m * 256, 256)
            for c0, w in ((IN2_MR, w_rnn_out_2), (IN2_MA, w_attn_out_2)):
                for m in range(4):
                    yield rows(w_in_2, 0, 8, c0 + m * 256, 256)
                    yield rows(w, 0, 8, m * 256, 256)
            for c in range(2):
                for r0 in (0, 4):
                    yield rows(w_o_2, r0, 4, c * 512, 512)

        block = ctx.enter_context(nc.Block())

        @block.sync
        def _(sp):
            xt = x.rearrange("o (t p) d -> p (o t) d", p=P)
            for t in range(TT):
                sp.dma_start(XTOK[:, t, :], xt[:, t, :]).then_inc(x_in[t], 16)
            for p, src in enumerate(transfers()):
                kd, ncol = src.shape[1], src.shape[2]
                if p >= 2:
                    sp.wait_ge(lo_done, 2 * p - 2)
                sp.dma_start(STAGE[:, p % 2, :].rearrange("p (k c) -> p k c", k=kd, c=ncol), src)\
                  .then_inc(landed[p % 2], 16)
                if p == 3:
                    sp.wait_ge(drained, KD)
                    sp.dma_start(XSCR, XCM[:].rearrange("p k s -> p (k s)")).then_inc(xscr_out, 16)
                if p == U_C // 2 + 6:
                    sp.wait_ge(xscr_out, 16)
                    sp.wait_ge(sc_done, HEADS)
                    sp.dma_start(X1[:].rearrange("p k s -> p (k s)"), XSCR).then_inc(xres_in, 16)
                if p == U_GR // 2 + 1:
                    sp.wait_ge(q2t_ready, KD + KVH)
                    sp.dma_start(LRUW[:, 0:KD, :], lru_w_a_2[0].rearrange("n c d -> c n d"))\
                      .then_inc(lruw_in, 16)
                    sp.dma_start(LRUW[:, KD:, :], lru_w_x_2[0].rearrange("n c d -> c n d"))\
                      .then_inc(lruw_in, 16)
                if p == U_H // 2 + 2:
                    sp.wait_ge(bd_done, KD)
                    sp.dma_start(FG[:], final_norm_g_2.partition_broadcast(P)).then_inc(fg_in, 16)
            for t in range(TT):
                sp.wait_ge(fin_ready, t + 1)
                sp.dma_start(out.rearrange("o (t p) d -> p (o t) d", p=P)[:, t, :], XT2[:, t, :])\
                  .then_inc(stored, 16)
            sp.wait_ge(stored, 16 * TT)

        @block.gpsimd
        def _(pool):
            n = 0

            def mask(t, fill, in_value, pattern, base, mult, op):
                nonlocal n
                pool.memset(t, in_value).then_inc(gchain, 1)
                n += 1
                pool.wait_ge(gchain, n)
                pool.affine_select(out=t, in_=t, compare_op=op, fill=fill, base=base,
                                   pattern=pattern, channel_multiplier=mult).then_inc(consts, 1)

            mask(IDENT[:], 0.0, 1.0, [[-1, P]], 0, 1, ALU.is_equal)
            pool.memset(ONES[:], 1.0).then_inc(consts, 1)
            pool.memset(SS[:], 0.0).then_inc(ss_clear, 1)
            mask(MINC[:], 0.0, 1.0, [[1, P]], 0, -1, ALU.is_ge)
            mask(NTRI[:], 0.0, -1.0, [[-1, P]], 0, 1, ALU.is_ge)
            pool.memset(NONE_[:], -1.0).then_inc(consts, 1)
            mask(MSTR[:], 0.0, 1.0, [[0, 2], [1, P]], 0, -1, ALU.is_gt)
            mask(MMIN[:], -BIG, BIG, [[0, 2], [1, P]], 0, -1, ALU.is_gt)
            pool.memset(CPAD[:, :, 0:32], 0.0).then_inc(consts, 1)

            def squares(e):
                for k in range(KD):
                    pool.wait_ge(sq_ready, KD * e + k + 1)
                    if k == 0:
                        pool.wait_ge(ss_clear, e + 1)
                    else:
                        pool.wait_ge(ss_added, KD * e + k)
                    pool.tensor_tensor(SS[:], SS[:], SQ[:], ALU.add).then_inc(ss_added, 1)
                if e < 2:
                    pool.wait_ge(stat_done, e + 1)
                    pool.memset(SS[:], 0.0).then_inc(ss_clear, 1)

            squares(0)
            squares(1)
            pool.wait_ge(merged, KD)
            pool.memset(UPB[:, :, 0:4], 0.0).then_inc(consts, 1)
            squares(2)
            pool.wait_ge(unit_done, U_G)
            pool.memset(AM[:, 0, :], -BIG).then_inc(gchain, 1)
            pool.memset(AM[:, 1:3, :], 0.0).then_inc(gchain, 1)
            n += 2
            pool.wait_ge(gchain, n)
            pool.affine_select(out=AM[:, 1, :], in_=AM[:, 1, :], compare_op=ALU.is_gt, fill=-BIG,
                               base=0, pattern=[[1, P]], channel_multiplier=-1).then_inc(consts, 1)
            pool.affine_select(out=AM[:, 2, :], in_=AM[:, 2, :], compare_op=ALU.is_ge, fill=-BIG,
                               base=0, pattern=[[-1, P]], channel_multiplier=1).then_inc(consts, 1)
            pool.memset(K2T[:, :, 0:P], 0.0).then_inc(consts, 1)
            pool.memset(UP2[:, :, 0:4], 0.0).then_inc(consts, 1)
            for m in range(KD // 2):
                pool.wait_ge(yg_sig, 2 * m + 2)
                pool.tensor_tensor(GT[:], GT[:], UP2[:, :, 4:516], ALU.mult).then_inc(yg_ready, 1)
                pool.wait_ge(yg_ready, m + 1)
                for c in (2 * m, 2 * m + 1):
                    pool.wait_ge(h_ready, c + 1)
                    pool.tensor_tensor(YR[:, c, :], YR[:, c, :], GT[:, c % 2, :], ALU.mult)\
                        .then_inc(yr_ready, 1)

        @block.scalar
        def _(act):
            def vec_rows(c, src):
                n, r = src.shape[0], c
                assert r // P == (r + n - 1) // P
                act.dma_start(ROWS[r % P:r % P + n, r // P, :], src).then_inc(vec_in, 16)

            def r128(v):
                return v.rearrange("(n p) -> n p", p=P)

            def dma_vectors():
                vec_rows(V_LN1, r128(ln1_g[0]))
                for j in range(2):
                    vec_rows(V_FW[j], r128(ffn_conv_w[0, j]))
                vec_rows(V_CW2, conv_w_2[0].rearrange("j (n p) -> (j n) p", p=P))
                vec_rows(V_CVW, cv_w[0].rearrange("j (n p) -> (j n) p", p=P))
                for i, g in enumerate((q_norm_g, k_norm_g)):
                    for h in range(2):
                        act.dma_start(ROWS[V_QKG + i:V_QKG + i + 1, 0, h * DH:(h + 1) * DH], g)\
                           .then_inc(vec_in, 16)
                vec_rows(V_FW[2], r128(ffn_conv_w[0, 2]))
                vec_rows(V_FB, r128(ffn_conv_b[0]))
                vec_rows(V_BG, b_gate[0].rearrange("j (n p) -> (j n) p", p=P))
                vec_rows(V_LN2, r128(ln2_g[0]))
                vec_rows(V_NG2, r128(norm_g_2[0]))
                for c, v in ((V_CVB, cv_b), (V_CLG, cv_ln_g), (V_CLB, cv_ln_b), (V_CB2, conv_b_2),
                             (V_BA, lru_b_a_2), (V_BX, lru_b_x_2), (V_LAM, lru_lambda_2)):
                    vec_rows(c, r128(v[0]))
                return 21

            act.wait_ge(vec_ready, 1)
            assert dma_vectors() == N_VEC
            act.dma_start(SGW[:], sg_w[0].rearrange("g t s -> t g s")).then_inc(sgw_in, 16)
            act.dma_start(SGLN[:, 0, :], sg_ln_g[0].partition_broadcast(P)).then_inc(bc_in, 16)
            act.dma_start(SGLN[:, 1, :], sg_ln_b[0].partition_broadcast(P)).then_inc(bc_in, 16)
            for g in range(8):
                act.dma_start(SGB[g % 2 * DH:(g % 2 + 1) * DH, g // 2, :],
                              sg_b[0, g].partition_broadcast(DH)).then_inc(bc_in, 16)
            act.dma_start(SINK[:], attn_sinks_2[0].partition_broadcast(P)).then_inc(bc_in, 16)
            act.dma_start(ROPE[:], rope.rearrange("(t p) c -> p t c", p=P)).then_inc(bc_in, 16)

            ns = 0

            def link(ins):
                nonlocal ns
                ins.then_inc(schain, 1)
                ns += 1
                act.wait_ge(schain, ns)

            def hi(n, i=0):
                act.wait_ge(landed[n // 2 % 2], 16 * (n // 4 + 1) + 16 * i)
                if n >= 4:
                    act.wait_ge(unit_done, n - 3 + 4 * i)
                act.activation(ring(WH, n), staged(n), ACT.Copy).then_inc(hi_done, 1)

            def feed(e, k, src, g, dr):
                act.wait_ge(drained, dr)
                act.activation(XH[:, k, :], src[:, k, :], ACT.Copy, scale=col(g + k))\
                   .then_inc(xh_ready, 1)
                if KD * e + k > 0:
                    act.wait_ge(ss_added, KD * e + k)
                act.activation(SQ[:], src[:, k, :], ACT.Square).then_inc(sq_ready, 1)

            def roots(e):
                act.wait_ge(ms_ready, 2 * e + 1)
                act.activation(RBC[:], RBC[:], ACT.Sqrt).then_inc(rt_ready, 1)
                act.wait_ge(ms_ready, 2 * e + 2)
                act.activation(SMALL[:, 0:TT], SMALL[:, 0:TT], ACT.Sqrt).then_inc(rt_ready, 1)

            hi(0)
            hi(1)
            act.wait_ge(vec_ready, 2)
            for k in range(KD):
                feed(0, k, XCM, V_LN1, k + 1)
                if k in (1, 3):
                    hi(2 + k // 2)
            roots(0)
            for n in range(U_A, U_B):
                hi(n + 4)
                j, t = divmod(n - 4, 4)
                if j in (0, 1):
                    act.wait_ge(drained, DR_A + 4 * j + t + 1)
                    if 4 * j + t > 0:
                        act.wait_ge(qk_red, 4 * j + t)
                    act.activation(TG1[:], QK[:, j, t, :], ACT.Square).then_inc(qk_sq, 1)
                if n == U_B - 4:
                    act.wait_ge(qk_ms, 1)
                    act.activation(SMALL[:, S_QKS:S_QKS + 64], SMALL[:, S_QKS:S_QKS + 64], ACT.Sqrt)\
                       .then_inc(qk_rt, 1)
                if j == 2:
                    act.wait_ge(drained, DR_A + 8 + t + 1)
                    act.activation(VSG[:, t, :], VSG[:, t, :], ACT.Gelu_apprx_tanh)\
                       .then_inc(vg_ready, 1)
            act.wait_ge(vg_var, 1)
            act.activation(SMALL[:, S_LN + 40:S_LN + 44], SMALL[:, S_LN + 40:S_LN + 44], ACT.Sqrt)\
               .then_inc(vg_sd, 1)
            for i in range(12):
                hi(U_B + i + 4)
                if i in (0, 1):
                    if i == 0:
                        act.wait_ge(xscr_out, 16)
                        act.wait_ge(vec_ready, 3)
                    for c in range(KW):
                        act.wait_ge(qkt_t, 4 * i + c + 1)
                        act.activation(QKT[:, i, c, :], PS[:, 2 + c, :], ACT.Copy,
                                       scale=col(V_QKG + i)).then_inc(qkt_ready, 1)
                h = i - 3
                if 0 <= h < HEADS:
                    b0 = 2 + 3 * (h % 2)
                    act.wait_ge(min_ready, 2 * h + 2)
                    if h > 0:
                        act.wait_ge(av_done, h)
                    act.activation(ABUF[:], PS[:, b0:b0 + 3, :].rearrange("p b c -> p (b c)")[:, 0:1280],
                                   ACT.Exp).then_inc(a_ready, 1)
                h = i - 2
                if 0 <= h < HEADS:
                    b0 = 2 + 3 * (h % 2)
                    act.wait_ge(sc_done, h + 1)
                    if h > 0:
                        act.wait_ge(sp_ready, 3 * h)
                    link(act.activation(E1[:], PS[:, b0:b0 + 3, :].rearrange("p b c -> p (b c)")[:, 0:1280],
                                        ACT.Abs))
                    link(act.activation(E1[:], E1[:], ACT.Exp, scale=-1.0))
                    act.activation(E1[:], E1[:], ACT.Ln, bias=1.0).then_inc(ln_ready, 1)
                if i in (2, 3, 6, 7, 8, 9, 10, 11):
                    act.wait_ge(drained, DR_B + i + 1)
                    t = (TG0, TG1)[i % 2]
                    act.activation(t[:], t[:], ACT.Sigmoid if i < 8 else ACT.Gelu_apprx_tanh)\
                       .then_inc(tg_act, 1)
            for b in range(3):
                if b == 0:
                    act.wait_ge(tg_used, 8)
                    act.wait_ge(av_done, HEADS)
                    src = UU
                elif b == 1:
                    act.wait_ge(att_read, HEADS)
                    src = ATT
                for q in range(2):
                    for r in range(6):
                        n = U_C + 12 * b + 6 * q + r
                        hi(n + 4)
                        if b < 2 and q == 0 and r == 0:
                            if b:
                                act.wait_ge(unit_done, n)
                            act.activation(BH[:], src[:], ACT.Copy).then_inc(bh_ready, 1)
                        if b == 2 and q == 0 and r == 1:
                            for c in range(KW):
                                act.wait_ge(c_cent, c + 1)
                                if c:
                                    act.wait_ge(c_ssum, c)
                                act.activation(TG1[:], CACC[:, c, :], ACT.Square).then_inc(c_sq, 1)
                        if r < 4:
                            act.wait_ge(drained, DR_C + 16 * b + 8 * q + r + 1)
                            act.activation(GS[:, r, :], GS[:, r, :], ACT.Sigmoid,
                                           bias=col(V_BG + BRANCHES[b] * KD + 4 * q + r))\
                               .then_inc(gs_ready, 1)
                        if b == 2 and q == 0 and r == 2:
                            act.wait_ge(c_ve, 1)
                            act.activation(TG0[:], TG0[:], ACT.Sqrt).then_inc(c_sd, 1)
                            for c in range(KW):
                                act.wait_ge(c_norm, c + 1)
                                act.activation(CACC[:, c, :], CACC[:, c, :], ACT.Silu,
                                               scale=col(V_CLG + c), bias=col(V_CLB + c))\
                                   .then_inc(c_ready, 1)
                            act.wait_ge(c_ready, KW)
                            act.activation(BH[:], CACC[:], ACT.Copy).then_inc(bh_ready, 1)
                    if b == 2 and q == 0:
                        for m in range(4):
                            act.wait_ge(merged, m + 1)
                            act.activation(MH[:, m, :], MERG[:, m, :], ACT.Copy).then_inc(mh_ready, 1)
            for m in range(4, KD):
                act.wait_ge(merged, m + 1)
                act.activation(MH[:, m, :], MERG[:, m, :], ACT.Copy).then_inc(mh_ready, 1)
            for m in range(KD):
                hi(U_D + m + 4)
                feed(1, m, X1, V_LN2, DR_D + m + 1)
            roots(1)

            def up_body(i, f0, last):
                f = f0 + i
                n = U_E + 4 * f0
                for r in range(4):
                    if last:
                        hi(n + 4 + r)
                    else:
                        hi(U_E + 4 + r + 4 * f0, i)
                    act.wait_ge(drained, DR_E + 4 * f + r + 1)
                    if f0 > 0:
                        act.wait_ge(gf_ready, 2 * f - 1 + r % 2)
                    c = r % 2 + (NF if r >= 2 else 0) + 2 * f
                    act.activation(YB[:, r, :], UPB[:, r, 4:516], ACT.Identity,
                                   scale=VEC[:, bass.ds(V_FW[2] + c, 1)],
                                   bias=VEC[:, bass.ds(V_FB + c, 1)]).then_inc(y_first, 1)
                    if r >= 2:
                        act.wait_ge(y_conv, 4 * f + r - 1)
                        act.activation(YB[:, r - 2, :], YB[:, r - 2, :], ACT.Silu)\
                           .then_inc(y_silu, 1)

            act.wait_ge(consts, 9)
            up_body(0, 0, False)
            with act.Fori(0, NF // 2 - 2) as i:
                up_body(i, 1, False)
            up_body(0, NF // 2 - 1, True)
            def ff_hi(kk):
                if kk >= 2:
                    act.wait_ge(unit_done, U_F + 2 * kk - 2)
                act.wait_ge(gf_ready, 2 * kk + 2)
                act.activation(FH[:, kk % 2], GF[:, 2 * kk:2 * kk + 2, :], ACT.Copy)\
                   .then_inc(fh_ready, 1)

            ff_hi(0)
            for kk in range(NF // 2):
                if kk < NF // 2 - 1:
                    ff_hi(kk + 1)
                hi(U_F + 2 * kk + 4)
                hi(U_F + 2 * kk + 5)
            for m in range(KD):
                feed(2, m, X1, V_NG2, DR_F + m + 1)
            roots(2)
            lam = SMALL[:, S_SP8:S_SP8 + KD]
            link(act.activation(lam, col(V_LAM, KD), ACT.Exp, scale=-1.0))
            link(act.activation(lam, lam, ACT.Ln, bias=1.0))
            act.activation(SMALL[:, S_NSP8:S_NSP8 + KD], lam, ACT.Copy, scale=-LRU_C)
            link(act.activation(lam, lam, ACT.Copy, scale=LRU_C))
            for i in range(12):
                hi(U_G + i + 4)
            for m in range(KD):
                hi(U_GA + m + 4)
                act.wait_ge(rt_t, m + 1 + max(0, m - 4))
                act.activation(Q2T[:, m, :], PS[:, 4 + m % 2, :], ACT.Copy).then_inc(q2t_ready, 1)
                if m >= 4:
                    act.wait_ge(rt_t, 2 * m - 2)
                    act.activation(K2T[:, m - 4, P:], PS[:, 6 + m % 2, :], ACT.Copy)\
                       .then_inc(q2t_ready, 1)
                act.wait_ge(drained, DR_GA + m + 1)
                act.activation(YA[:, m, :], YA[:, m, :], ACT.Silu).then_inc(ya_silu, 1)

            def window_exp(s):
                buf = S2[s % 2]
                act.wait_ge(s2_max, s + 1)
                for par in range(2):
                    for idx in range(2):
                        j = 2 * par + idx
                        act.activation(buf[:, par, idx, :], buf[:, par, idx, :], ACT.Exp,
                                       bias=SMALL[:, S_ATT + 4 + j:S_ATT + 5 + j],
                                       accum_out=SMALL[:, S_ATT + 12 + j:S_ATT + 13 + j])\
                           .then_inc(s2_exp, 1)
                act.activation(SMALL[:, S_ATT + 8:S_ATT + 12], SMALL[:, S_ATT + 8:S_ATT + 12],
                               ACT.Exp).then_inc(s2_exp, 1)

            def window_pt(s):
                act.wait_ge(pt_t, s + 1)
                if s > 0:
                    act.wait_ge(pv_done, s)
                act.activation(PT[:].rearrange("p a b c d -> p (a b c d)"),
                               PS[:, 4:6, :].rearrange("p b c -> p (b c)"), ACT.Copy)\
                   .then_inc(pt_ready, 1)

            def first_tap(c):
                act.wait_ge(drained, DR_GR + 4 * (c // 2) + c % 2 + 1)
                if c >= 2:
                    act.wait_ge(iu_ready, c - 1)
                    act.wait_ge(bsq_ready, c - 1)
                act.activation(UC[c % 2][:], UP2[:, c % 2, 4:516], ACT.Identity,
                               scale=col(V_CW2 + 3 * KD + c), bias=col(V_CB2 + c))\
                   .then_inc(uc_first, 1)

            def rec_sigmoid(c):
                act.wait_ge(bd_done, c + 1)
                if c >= 2:
                    act.wait_ge(h_ready, c - 1)
                act.activation(RR[c % 2][:], PS[:, 2, :], ACT.Sigmoid, bias=col(V_BA + c))\
                   .then_inc(gate_ri, 1)
                act.activation(II[c % 2][:], PS[:, 3, :], ACT.Sigmoid, bias=col(V_BX + c))\
                   .then_inc(gate_ri, 1)

            def rec_exp(c):
                act.wait_ge(gate_ri, 2 * c + 2)
                act.activation(YR[:, c, :], RR[c % 2][:], ACT.Exp,
                               scale=SMALL[:, S_NSP8 + c:S_NSP8 + c + 1]).then_inc(a_exp, 1)
                act.activation(RR[c % 2][:], RR[c % 2][:], ACT.Tanh,
                               scale=SMALL[:, S_SP8 + c:S_SP8 + c + 1]).then_inc(tanh_ready, 1)

            def rec_root(c):
                act.wait_ge(bsq_ready, c + 1)
                act.activation(RR[c % 2][:], RR[c % 2][:], ACT.Sqrt).then_inc(bsqrt, 1)

            act.wait_ge(consts, 13)
            for s in range(16 + 3):
                m, q = divmod(s, 4)
                if s < 16:
                    hi(U_GR + s + 4)
                if 2 <= s < 18:
                    window_pt(s - 2)
                if q in (1, 2) and s < 16:
                    first_tap(2 * m + q - 1)
                if q == 0 and m:
                    rec_sigmoid(2 * m - 1)
                    rec_exp(2 * m - 2)
                    rec_exp(2 * m - 1)
                if s < 16:
                    window_exp(s)
                if q == 1 and m:
                    rec_root(2 * m - 2)
                    rec_root(2 * m - 1)
                if q == 3 and s < 16:
                    rec_sigmoid(2 * m)
                    for c in (2 * m, 2 * m + 1):
                        act.wait_ge(drained, DR_GR + 4 * m + 2 + c % 2 + 1)
                        if c % 2 == 0:
                            act.wait_ge(uc_ready, 2 * m + 2)
                        act.activation(UP2[:, c % 2, 4:516], GT[:, c % 2, :], ACT.Sigmoid)\
                           .then_inc(yg_sig, 1)
            for i in range(8):
                if i == 0:
                    act.wait_ge(qk2_done, 16)
                    for k in range(KD):
                        act.wait_ge(yr_ready, k + 1)
                        act.activation(BH2[:, k, :], YR[:, k, :], ACT.Copy).then_inc(bh2_ready, 1)
                if i == 4:
                    act.wait_ge(unit_done, U_H + 16)
                    act.wait_ge(pv_read, 16)
                    for k in range(KD):
                        act.activation(BH2[:, k, :], YA[:, k, :], ACT.Copy).then_inc(bh2_ready, 1)
                for r in range(4):
                    hi(U_H + 4 * i + r + 4)
                    if r < 2:
                        act.wait_ge(drained, DR_H + 4 * i + r + 1)
                        act.activation(GS2[:, r, :], GS2[:, r, :], ACT.Sigmoid).then_inc(gs2_ready, 1)
                if i >= 4:
                    for m in (2 * i - 8, 2 * i - 7):
                        act.wait_ge(merged2, m + 1)
                        act.activation(M2H[:, m, :], MERG2[:, m, :], ACT.Copy).then_inc(m2h_ready, 1)
            for t in range(TT):
                act.wait_ge(x2t_t, t + 1)
                act.activation(XT2[:, t, :], PS[:, 4 + 2 * (t % 2):6 + 2 * (t % 2), :]
                               .rearrange("p b c -> p (b c)"), ACT.Copy).then_inc(x2t_ready, 1)
            for i in range(4):
                hi(U_O + i + 4)
            for t in range(TT):
                act.wait_ge(drained, DR_O + 4 + t + 1)
                if t:
                    act.wait_ge(fin_sq, t)
                act.activation(SQF[:], XT2[:, t, :], ACT.Square,
                               accum_out=SMALL[:, S_FIN + t:S_FIN + t + 1]).then_inc(fin_sq, 1)
            for t in range(TT):
                act.wait_ge(fin_ms, t + 1)
                act.activation(SMALL[:, S_FIN + t:S_FIN + t + 1], SMALL[:, S_FIN + t:S_FIN + t + 1],
                               ACT.Sqrt).then_inc(fin_sd, 1)

        @block.vector
        def _(dve):
            nv = 0

            def link(ins):
                nonlocal nv
                ins.then_inc(vchain, 1)
                nv += 1
                dve.wait_ge(vchain, nv)

            def lo(n, i=0):
                dve.wait_ge(hi_done, n + 1 + 4 * i)
                dve.tensor_tensor(ring(WL, n), staged(n), ring(WH, n).bitcast(F32), ALU.subtract)\
                   .then_inc(lo_done, 1)

            def feed(e, k, src, g):
                dve.wait_ge(xh_ready, KD * e + k + 1)
                dve.scalar_tensor_tensor(XL[:, k, :], src[:, k, :], col(g + k),
                                         XH[:, k, :].bitcast(F32), ALU.mult, ALU.subtract)\
                   .then_inc(xl_ready, 1)

            def norm(e):
                dve.wait_ge(stat_done, e + 1)
                dve.tensor_scalar(RBC[:], PS[:, 7, :], 1.0 / D, EPS, ALU.mult, ALU.add)\
                   .then_inc(ms_ready, 1)
                dve.tensor_scalar(SMALL[:, 0:TT], PS[:, 6, 0:TT], 1.0 / D, EPS, ALU.mult, ALU.add)\
                   .then_inc(ms_ready, 1)
                dve.wait_ge(rt_ready, 2 * e + 2)
                dve.reciprocal(SMALL[:, 0:TT], SMALL[:, 0:TT]).then_inc(r_ready, 1)
                dve.reciprocal(RBC[:], RBC[:]).then_inc(r_ready, 1)

            def rtok(t):
                return SMALL[:, t:t + 1]

            dve.memset(ROWS[:], 0.0).then_inc(vec_ready, 1)
            dve.wait_ge(vec_t, 1)
            dve.tensor_copy(VEC[:], PS[:, 0, :]).then_inc(vec_ready, 1)
            dve.wait_ge(vec_ready, 2)
            dve.tensor_scalar(col(V_QKG), col(V_QKG), DH ** -0.5, None, ALU.mult)\
               .then_inc(vec_ready, 1)
            for k in range(KD):
                dve.wait_ge(xt_done, k + 1)
                dve.tensor_copy(XCM[:, k, :], PS[:, k, :]).then_inc(drained, 1)
                dve.wait_ge(drained, k + 1)
                feed(0, k, XCM, V_LN1)
                if k in (1, 3):
                    lo(k - 1)
                    lo(k)
            norm(0)
            dve.wait_ge(r_ready, 2)
            ssq = SMALL[:, S_QKS:S_QKS + 64]
            for n in range(U_A, U_B + 4):
                j, t = divmod(n - 4, 4)
                if n < U_B:
                    lo(n + 4)
                if n >= 4:
                    if t == 0:
                        dve.wait_ge(unit_done, U_A + 4 * j + 4)
                    dst = (QK[:, 0, t, :], QK[:, 1, t, :], VSG[:, t, :], VATT[:, t, :])[j]
                    dve.tensor_scalar(dst, PS[:, 4 * (j % 2) + t, :], rtok(t), None, ALU.mult)\
                       .then_inc(drained, 1)
                if 0 <= j < 2:
                    dve.wait_ge(qk_sq, 4 * j + t + 1)
                    dve.tensor_reduce(SMALL[:, S_QKS + 8 * (4 * j + t):S_QKS + 8 * (4 * j + t) + 8],
                                      TG1[:].rearrange("p (h d) -> p h d", d=DH), AX.X, ALU.add)\
                       .then_inc(qk_red, 1)
                if n == U_B - 5:
                    dve.wait_ge(qk_red, 8)
                    dve.tensor_scalar(ssq, ssq, 1.0 / DH, EPS, ALU.mult, ALU.add).then_inc(qk_ms, 1)
                if n == U_B - 3:
                    dve.wait_ge(qk_rt, 1)
                    link(dve.reciprocal(ssq, ssq))
                    for i in range(2):
                        for tt in range(TT):
                            c = S_QKS + 8 * (4 * i + tt)
                            v = QK[:, i, tt, :].rearrange("p (h d) -> p h d", d=DH)
                            dve.tensor_tensor(v, v, SMALL[:, c:c + 8].unsqueeze(2)
                                              .broadcast_to([P, HEADS, DH]), ALU.mult)\
                               .then_inc(qk_ready, 1)
                if n == U_B:
                    dve.wait_ge(bc_in, 16 * 12)
                    for tt in range(TT):
                        dve.wait_ge(vg_ready, tt + 1)
                        dve.bn_stats(SMALL[:, S_LN + 6 * tt:S_LN + 6 * tt + 6], VSG[:, tt, :])\
                           .then_inc(vchain, 1)
                        nv += 1
                    dve.wait_ge(vchain, nv)
                    for tt in range(TT):
                        dve.bn_aggr(SMALL[:, S_LN + 24 + 2 * tt:S_LN + 26 + 2 * tt],
                                    SMALL[:, S_LN + 6 * tt:S_LN + 6 * tt + 6]).then_inc(vchain, 1)
                        nv += 1
                    dve.wait_ge(vchain, nv)
                    var = SMALL[:, S_LN + 24:S_LN + 32].rearrange("p (t two) -> p t two", two=2)[:, :, 1]
                    dve.tensor_scalar(SMALL[:, S_LN + 40:S_LN + 44], var, EPS, None, ALU.add)\
                       .then_inc(vg_var, 1)
            dve.wait_ge(vg_sd, 1)
            sd = SMALL[:, S_LN + 40:S_LN + 44]
            link(dve.reciprocal(sd, sd))
            for tt in range(TT):
                link(dve.tensor_scalar(VSG[:, tt, :], VSG[:, tt, :],
                                       SMALL[:, S_LN + 24 + 2 * tt:S_LN + 25 + 2 * tt],
                                       SMALL[:, S_LN + 40 + tt:S_LN + 41 + tt],
                                       ALU.subtract, ALU.mult))
                link(dve.tensor_tensor(VSG[:, tt, :], VSG[:, tt, :], SGLN[:, 0, :], ALU.mult))
                dve.tensor_tensor(VSG[:, tt, :], VSG[:, tt, :], SGLN[:, 1, :], ALU.add)\
                   .then_inc(vn_ready, 1)
            taps_done = 0

            def taps(k):
                nonlocal taps_done
                for _ in range(k):
                    if taps_done == CVK * KW:
                        return
                    j, c = divmod(taps_done, KW)
                    if j == 0:
                        ins = dve.tensor_scalar(CACC[:, c, :], CPAD[:, c, 2:2 + SEQ], col(V_CVW + c),
                                                col(V_CVB + c), ALU.mult, ALU.add)
                    else:
                        dve.wait_ge(c_tap, taps_done - KW + 1)
                        ins = dve.scalar_tensor_tensor(
                            CACC[:, c, :], CPAD[:, c, 2 + j:2 + j + SEQ], col(V_CVW + KW * j + c),
                            CACC[:, c, :], ALU.mult, ALU.add)
                    ins.then_inc(c_tap, 1)
                    taps_done += 1

            tg_jobs = {2: CPAD[:, 0, 32:], 3: CPAD[:, 1, 32:], 6: CPAD[:, 2, 32:],
                       7: CPAD[:, 3, 32:], 8: UU[:, 0, :], 9: UU[:, 1, :], 10: UU[:, 2, :],
                       11: UU[:, 3, :]}
            tg_order = sorted(tg_jobs)

            def tg_mult(i):
                if i in tg_jobs:
                    k = tg_order.index(i)
                    dve.wait_ge(tg_act, k + 1)
                    dve.tensor_tensor(tg_jobs[i], tg_jobs[i], (TG0, TG1)[i % 2][:], ALU.mult)\
                       .then_inc(tg_used, 1)

            for i in range(12):
                dve.wait_ge(unit_done, U_B + i + 1)
                if i in (0, 1, 4, 5):
                    c = i % 4 + (2 if i >= 4 else 0)
                    dst = CPAD[:, c, 32:]
                else:
                    dst = (TG0, TG1)[i % 2][:]
                    if i >= 6:
                        dve.wait_ge(tg_used, tg_order.index(i) - 1)
                dve.tensor_tensor(dst, PS[:, i % 2, :], RBC[:], ALU.mult).then_inc(drained, 1)
                tg_mult(i - 1)
                h = i - 4
                if 0 <= h < HEADS:
                    rows_ = slice(DH * (h % 2), DH * (h % 2) + DH)
                    dve.wait_ge(av_done, h + 1)
                    dve.tensor_copy(ATT[rows_, h // 2, :], PS[rows_, 2 + 3 * (h % 2), :])\
                       .then_inc(att_read, 1)
                h = i - 3
                if 0 <= h < HEADS:
                    b0 = 2 + 3 * (h % 2)
                    dve.wait_ge(tri_done, h + 1)
                    z = PS[:, b0:b0 + 2, 0:P]
                    dve.tensor_tensor(z, z, MMIN[:], ALU.min).then_inc(min_ready, 1)
                    z = PS[:, b0:b0 + 3, :].rearrange("p b c -> p (b c)")[:, 896:1152]
                    dve.tensor_tensor(z, z, MMIN[:].rearrange("p a c -> p (a c)"), ALU.min)\
                       .then_inc(min_ready, 1)
                if i == 0:
                    for q in range(2):
                        dve.wait_ge(wt_t, q + 1)
                        dve.tensor_tensor(WT[:, 4 * q:4 * q + 4, :],
                                          PS[:, 6 + q, :].rearrange("p (g t) -> p g t", t=P),
                                          MINC[:].unsqueeze(1).broadcast_to([P, 4, P]), ALU.mult)\
                           .then_inc(wt_ready, 1)
                lo(U_B + i + 4)
                if i in (1, 2):
                    for c in (2 * i - 2, 2 * i - 1):
                        dve.wait_ge(sg_done, c + 1)
                        dve.tensor_tensor(UU[:, c, :].rearrange("p (n t) -> p n t", t=P),
                                          PS[:, 6 + c % 2, :].rearrange("p (n t) -> p n t", t=P),
                                          SGB[:, c, :].unsqueeze(1).broadcast_to([P, TT, P]), ALU.add)\
                           .then_inc(sg_read, 1)
                h = i - 2
                if 0 <= h < HEADS:
                    b0 = 2 + 3 * (h % 2)
                    dve.wait_ge(ln_ready, h + 1)
                    if h:
                        dve.wait_ge(tri_done, h)
                    dve.scalar_tensor_tensor(
                        SPB[:], PS[:, b0:b0 + 3, :].rearrange("p b c -> p (b c)")[:, 0:1280], 0.0, E1[:],
                        ALU.max, ALU.add).then_inc(sp_ready, 1)
                    dve.wait_ge(sp_ready, 3 * h + 1)
                    z = SPB[:, 0:1024].rearrange("p (a c) -> p a c", a=2)[:, :, 0:P]
                    dve.tensor_tensor(z, z, MSTR[:], ALU.mult).then_inc(sp_ready, 1)
                    z = SPB[:, 896:1152]
                    dve.tensor_tensor(z, z, MSTR[:].rearrange("p a c -> p (a c)"), ALU.mult)\
                       .then_inc(sp_ready, 1)
                if i >= 9:
                    taps(4)
            tg_mult(11)
            for b in range(3):
                for q in range(2):
                    for r in range(6):
                        n = U_C + 12 * b + 6 * q + r
                        dve.wait_ge(unit_done, n + 1)
                        if r < 4:
                            dve.tensor_tensor(GS[:, r, :], PS[:, r, :], RBC[:], ALU.mult)\
                               .then_inc(drained, 1)
                        lo(n + 4)
                        if r == 5:
                            for m in range(4):
                                mm = 4 * q + m
                                dve.wait_ge(gs_ready, 8 * b + 4 * q + m + 1)
                                dst = MERG[:, mm, :] if b == 0 else TMPY[:]
                                if b == 2 and mm:
                                    dve.wait_ge(merged, mm)
                                dve.tensor_tensor(dst, PS[:, 4 + m, :], GS[:, m, :], ALU.mult)\
                                   .then_inc(drained, 1)
                                if b:
                                    dve.wait_ge(drained, DR_C + 16 * b + 8 * q + 4 + m + 1)
                                    ins = dve.tensor_tensor(MERG[:, mm, :], MERG[:, mm, :], TMPY[:],
                                                            ALU.add)
                                    if b == 2:
                                        ins.then_inc(merged, 1)
                                    else:
                                        link(ins)
                        if b < 2 and q == 0 and r == 0:
                            src = (UU, ATT)[b]
                            dve.wait_ge(bh_ready, b + 1)
                            dve.tensor_tensor(BL[:], src[:], BH[:].bitcast(F32), ALU.subtract)\
                               .then_inc(bl_ready, 1)
                        if b < 2:
                            taps(5)
                        if b == 1 and q == 1 and r == 5:
                            assert taps_done == CVK * KW
                            dve.wait_ge(c_tap, CVK * KW)
                            link(dve.tensor_tensor(TG1[:], CACC[:, 0, :], CACC[:, 1, :], ALU.add))
                            link(dve.tensor_tensor(TG0[:], CACC[:, 2, :], CACC[:, 3, :], ALU.add))
                            dve.tensor_tensor(TG1[:], TG1[:], TG0[:], ALU.add).then_inc(c_sum, 1)
                        if b == 2 and q == 0 and r == 0:
                            dve.wait_ge(c_mean, 1)
                            for c in range(KW):
                                dve.scalar_tensor_tensor(CACC[:, c, :], PS[:, 4, :], -1.0 / W,
                                                         CACC[:, c, :], ALU.mult, ALU.add)\
                                   .then_inc(c_cent, 1)
                        if b == 2 and q == 0 and r == 1:
                            for c in range(KW):
                                dve.wait_ge(c_sq, c + 1)
                                if c:
                                    dve.wait_ge(c_ssum, c)
                                    ins = dve.tensor_tensor(TG0[:], TG0[:], TG1[:], ALU.add)
                                else:
                                    ins = dve.tensor_copy(TG0[:], TG1[:])
                                ins.then_inc(c_ssum, 1)
                        if b == 2 and q == 0 and r == 2:
                            dve.wait_ge(c_var, 1)
                            dve.tensor_scalar(TG0[:], PS[:, 5, :], 1.0 / W, EPS, ALU.mult, ALU.add)\
                               .then_inc(c_ve, 1)
                            dve.wait_ge(c_sd, 1)
                            link(dve.reciprocal(TG0[:], TG0[:]))
                            for c in range(KW):
                                dve.tensor_tensor(CACC[:, c, :], CACC[:, c, :], TG0[:], ALU.mult)\
                                   .then_inc(c_norm, 1)
                            dve.wait_ge(bh_ready, 3)
                            dve.tensor_tensor(BL[:], CACC[:], BH[:].bitcast(F32), ALU.subtract)\
                               .then_inc(bl_ready, 1)
                    if b == 2:
                        for m in range(4 * q, 4 * q + 4):
                            dve.wait_ge(mh_ready, m + 1)
                            dve.tensor_tensor(ML[:, m, :], MERG[:, m, :], MH[:, m, :].bitcast(F32),
                                              ALU.subtract).then_inc(ml_ready, 1)
            dve.wait_ge(xres_in, 16)
            for m in range(KD):
                dve.wait_ge(unit_done, U_D + m + 1)
                dve.tensor_tensor(X1[:, m, :], PS[:, m % 4, :], X1[:, m, :], ALU.add)\
                   .then_inc(drained, 1)
                dve.wait_ge(drained, DR_D + m + 1)
                feed(1, m, X1, V_LN2)
                lo(U_D + m + 4)
            norm(1)
            dve.wait_ge(r_ready, 4)
            dve.wait_ge(consts, 9)

            def up_conv(r, f0, i):
                c = r % 2 + (NF if r >= 2 else 0) + 2 * f0 + 2 * i
                dve.wait_ge(y_first, 4 * f0 + r + 1 + 4 * i)
                dve.scalar_tensor_tensor(YB[:, r, :], UPB[:, r, 3:515], VEC[:, bass.ds(V_FW[1] + c, 1)],
                                         YB[:, r, :], ALU.mult, ALU.add).then_inc(y_tap, 1)
                dve.wait_ge(y_tap, 4 * f0 + r + 1 + 4 * i)
                dve.scalar_tensor_tensor(YB[:, r, :], UPB[:, r, 2:514], VEC[:, bass.ds(V_FW[0] + c, 1)],
                                         YB[:, r, :], ALU.mult, ALU.add).then_inc(y_conv, 1)

            def up_body(i, f0, last):
                for r in range(4):
                    dve.wait_ge(unit_done, U_E + 4 * f0 + r + 1 + 4 * i)
                    dve.tensor_tensor(UPB[:, r, 4:516], PS[:, r, :], RBC[:], ALU.mult)\
                       .then_inc(drained, 1)
                    if r:
                        up_conv(r - 1, f0, i)
                    if last:
                        lo(U_E + 4 * f0 + r + 4)
                    else:
                        lo(U_E + 4 * f0 + 4 + r, i)
                up_conv(3, f0, i)
                for r in range(2):
                    dve.wait_ge(y_silu, 2 * f0 + r + 1 + 2 * i)
                    if r == 0:
                        dve.wait_ge(y_conv, 4 * f0 + 4 + 4 * i)
                    dve.tensor_tensor(GF[:, bass.ds(2 * f0 + r + 2 * i, 1), :],
                                      YB[:, r:r + 1, :], YB[:, r + 2:r + 3, :], ALU.mult)\
                       .then_inc(gf_ready, 1)

            up_body(0, 0, False)
            with dve.Fori(0, NF // 2 - 2) as i:
                up_body(i, 1, False)
            up_body(0, NF // 2 - 1, True)
            def ff_lo(kk):
                dve.wait_ge(fh_ready, kk + 1)
                dve.tensor_tensor(FL[:, kk % 2], GF[:, 2 * kk:2 * kk + 2, :], FH[:, kk % 2].bitcast(F32),
                                  ALU.subtract).then_inc(fl_ready, 1)

            ff_lo(0)
            for kk in range(NF // 2):
                if kk < NF // 2 - 1:
                    ff_lo(kk + 1)
                lo(U_F + 2 * kk + 4)
                lo(U_F + 2 * kk + 5)
            for m in range(KD):
                if m % 4 == 0:
                    dve.wait_ge(unit_done, U_G - 1 + m // 4)
                dve.tensor_tensor(X1[:, m, :], PS[:, m, :], X1[:, m, :], ALU.add).then_inc(drained, 1)
                dve.wait_ge(drained, DR_F + m + 1)
                feed(2, m, X1, V_NG2)
            norm(2)
            dve.wait_ge(r_ready, 6)
            for j in range(3):
                for t in range(TT):
                    if j == 0:
                        lo(U_G + t + 4)
                for t in range(TT):
                    if t == 0:
                        dve.wait_ge(unit_done, U_G + 4 * j + 4)
                    if j < 2:
                        dve.tensor_scalar(Q2[:, t, 512 * j:512 * j + 512], PS[:, t, :], rtok(t),
                                          DH ** -0.5, ALU.mult, ALU.mult).then_inc(drained, 1)
                    else:
                        dve.tensor_scalar(KDUP[:, t, :, 0:DH],
                                          PS[:, t, 0:256].rearrange("p (g d) -> p g d", d=DH),
                                          rtok(t), None, ALU.mult)
                        dve.tensor_scalar(V2[:, t, :], PS[:, t, 256:512], rtok(t), None, ALU.mult)\
                           .then_inc(drained, 1)
                if j < 2:
                    for t in range(TT):
                        lo(U_G + 4 * j + t + 8)
            dve.wait_ge(drained, DR_G + 12)
            for v, nh in ((Q2[:].rearrange("p t (h d) -> p t h d", d=DH), 16),
                          (KDUP[:], KVH)):
                a, b2 = v[:, :, :, 0:8], v[:, :, :, 8:16]
                cos = ROPE[:, :, 0:8].unsqueeze(2).broadcast_to([P, TT, nh, 8])
                sin = ROPE[:, :, 8:16].unsqueeze(2).broadcast_to([P, TT, nh, 8])
                r_ = [RT[:, z, 0:TT * nh * 8].rearrange("p (t h d) -> p t h d", t=TT, h=nh)
                      for z in range(4)]
                if nh == KVH:
                    dve.wait_ge(rope_ready, 2)
                dve.tensor_tensor(r_[0], a, cos, ALU.mult)
                dve.tensor_tensor(r_[1], b2, sin, ALU.mult)
                dve.tensor_tensor(r_[2], b2, cos, ALU.mult)
                link(dve.tensor_tensor(r_[3], a, sin, ALU.mult))
                dve.tensor_tensor(a, r_[0], r_[1], ALU.subtract).then_inc(rope_ready, 1)
                dve.tensor_tensor(b2, r_[2], r_[3], ALU.add).then_inc(rope_ready, 1)
            dve.wait_ge(rope_ready, 4)
            dve.tensor_copy(KDUP[:, :, :, DH:], KDUP[:, :, :, 0:DH]).then_inc(rope_ready, 1)
            for m in range(KD):
                dve.wait_ge(unit_done, U_GA + m + 1)
                dve.tensor_tensor(YA[:, m, :], PS[:, m % 2, :], RBC[:], ALU.mult).then_inc(drained, 1)
                lo(U_GA + m + 4)

            def window_read(s):
                g, nb = divmod(s, TT)
                dve.wait_ge(pv_done, s + 1)
                ya = YA[:, 2 * g:2 * g + 2, nb * P:(nb + 1) * P]
                dve.tensor_tensor(ya, PS[:, 6, 0:256].rearrange("p (i q) -> p i q", q=P), ya, ALU.mult)\
                   .then_inc(pv_read, 1)

            def att(c, n=4):
                return SMALL[:, S_ATT + c:S_ATT + c + n]

            def window_max(s):
                g, nb = divmod(s, TT)
                buf = S2[s % 2]
                dve.wait_ge(qk2_done, s + 1)
                if s >= 2:
                    dve.wait_ge(pt_t, s - 1)
                mask = AM[:, 1:3, :] if nb else AM[:, 0:3:2, :]
                for par in range(2):
                    dve.tensor_tensor(buf[:, par].rearrange("p i (b c) -> p i b c", b=2),
                                      PS[:, 6 + par, :].rearrange("p (i b c) -> p i b c", i=2, b=2),
                                      mask.unsqueeze(1).broadcast_to([P, 2, 2, P]),
                                      ALU.add).then_inc(s2_mask, 1)
                dve.wait_ge(s2_mask, 2 * s + 2)
                link(dve.tensor_reduce(att(0).rearrange("p (a b) -> p a b", a=2), buf[:], AX.X, ALU.max))
                sink = SINK[:, 4 * g:4 * g + 4].rearrange("p (i a) -> p a i", a=2)
                m2 = att(0).rearrange("p (a b) -> p a b", a=2)
                link(dve.tensor_tensor(m2, m2, sink, ALU.max))
                dve.tensor_scalar(att(4), att(0), -1.0, None, ALU.mult)
                dve.tensor_tensor(att(8).rearrange("p (a b) -> p a b", a=2), sink, m2, ALU.subtract)\
                   .then_inc(s2_max, 1)

            def window_norm(s):
                dve.wait_ge(s2_exp, 5 * s + 5)
                link(dve.tensor_tensor(att(16), att(12), att(8), ALU.add))
                link(dve.reciprocal(att(16), att(16)))
                v = S2[s % 2][:].rearrange("p a b c -> p (a b) c")
                dve.tensor_tensor(v, v, att(16).unsqueeze(2).broadcast_to([P, 4, 256]), ALU.mult)\
                   .then_inc(s2_ready, 1)

            def rec_conv(c):
                dve.wait_ge(uc_first, c + 1)
                for j in (2, 1, 0):
                    ins = dve.scalar_tensor_tensor(
                        UC[c % 2][:], UP2[:, c % 2, 1 + j:1 + j + SEQ], col(V_CW2 + KD * j + c),
                        UC[c % 2][:], ALU.mult, ALU.add)
                    if j:
                        link(ins)
                    else:
                        ins.then_inc(uc_ready, 1)

            def rec_input(c):
                dve.wait_ge(gate_ri, 2 * c + 2)
                dve.tensor_tensor(II[c % 2][:], II[c % 2][:], UC[c % 2][:], ALU.mult)\
                   .then_inc(iu_ready, 1)

            def rec_square(c):
                dve.wait_ge(a_exp, c + 1)
                dve.wait_ge(tanh_ready, c + 1)
                dve.wait_ge(iu_ready, c + 1)
                link(dve.tensor_tensor(UC[c % 2][:], YR[:, c, :], YR[:, c, :], ALU.mult))
                dve.scalar_tensor_tensor(RR[c % 2][:], UC[c % 2][:], 1.0, RR[c % 2][:], ALU.add,
                                         ALU.mult).then_inc(bsq_ready, 1)

            def rec_scan(c):
                dve.wait_ge(bsqrt, c + 1)
                link(dve.tensor_tensor(RR[c % 2][:], RR[c % 2][:], II[c % 2][:], ALU.mult))
                dve.tensor_tensor_scan(YR[:, c, :], YR[:, c, :], RR[c % 2][:], 0.0, ALU.mult, ALU.add)\
                   .then_inc(h_ready, 1)

            dve.wait_ge(consts, 13)
            dve.wait_ge(ya_silu, KD)
            for s in range(19):
                m, q = divmod(s, 4)
                if s < 16:
                    dve.wait_ge(unit_done, U_GR + s + 1)
                    if q < 2:
                        dst = UP2[:, q, 4:516]
                        if m:
                            dve.wait_ge(yg_ready, m)
                    else:
                        dst = GT[:, q - 2, :]
                        if m:
                            dve.wait_ge(yr_ready, 2 * m)
                    dve.tensor_tensor(dst, PS[:, s % 2, :], RBC[:], ALU.mult).then_inc(drained, 1)
                if s >= 3:
                    window_read(s - 3)
                if s < 16:
                    lo(U_GR + s + 4)
                if q == 0 and m:
                    rec_input(2 * m - 2)
                if s < 16:
                    window_max(s)
                if q in (1, 2) and s < 16:
                    rec_conv(2 * m + q - 1)
                if s < 16:
                    window_norm(s)
                if q == 0 and m:
                    rec_input(2 * m - 1)
                    rec_square(2 * m - 2)
                    rec_square(2 * m - 1)
                if q == 1 and m:
                    rec_scan(2 * m - 2)
                    rec_scan(2 * m - 1)
            for i in range(8):
                if i in (0, 4):
                    src = YR if i == 0 else YA
                    if i == 4:
                        dve.wait_ge(pv_read, 16)
                    for k in range(KD):
                        dve.wait_ge(bh2_ready, 2 * i + k + 1)
                        dve.tensor_tensor(BL2[:, k, :], src[:, k, :], BH2[:, k, :].bitcast(F32),
                                          ALU.subtract).then_inc(bl2_ready, 1)
                for r in range(4):
                    n = U_H + 4 * i + r
                    dve.wait_ge(unit_done, n + 1)
                    if r < 2:
                        if i:
                            dve.wait_ge(drained, DR_H + 4 * i + r - 1)
                        dve.tensor_tensor(GS2[:, r, :], PS[:, r, :], RBC[:], ALU.mult)\
                           .then_inc(drained, 1)
                    else:
                        m = 2 * (i % 4) + r - 2
                        dve.wait_ge(gs2_ready, 2 * i + r - 1)
                        dst = MERG2[:, m, :] if i < 4 else TMP2[:]
                        if i >= 4 and m:
                            dve.wait_ge(merged2, m)
                        dve.tensor_tensor(dst, PS[:, r, :], GS2[:, r - 2, :], ALU.mult)\
                           .then_inc(drained, 1)
                        if i >= 4:
                            dve.wait_ge(drained, DR_H + 4 * i + r + 1)
                            dve.tensor_tensor(MERG2[:, m, :], MERG2[:, m, :], TMP2[:], ALU.add)\
                               .then_inc(merged2, 1)
                    lo(n + 4)
                if i >= 4:
                    for m in (2 * i - 8, 2 * i - 7):
                        dve.wait_ge(m2h_ready, m + 1)
                        dve.tensor_tensor(M2L[:, m, :], MERG2[:, m, :], M2H[:, m, :].bitcast(F32),
                                          ALU.subtract).then_inc(m2l_ready, 1)
            for i in range(4):
                lo(U_O + i + 4)
            for c in range(2):
                dve.wait_ge(unit_done, U_O + 4 * c + 4)
                for t in range(TT):
                    dve.wait_ge(x2t_ready, t + 1)
                    v = XT2[:, t, c * 512:c * 512 + 512]
                    dve.tensor_tensor(v, PS[:, 4 * c + t, :], v, ALU.add).then_inc(drained, 1)
            dve.wait_ge(fg_in, 16)
            for t in range(TT):
                s_ = SMALL[:, S_FIN + t:S_FIN + t + 1]
                dve.wait_ge(fin_sq, t + 1)
                dve.tensor_scalar(s_, s_, 1.0 / D, EPS, ALU.mult, ALU.add).then_inc(fin_ms, 1)
            for t in range(TT):
                s_ = SMALL[:, S_FIN + t:S_FIN + t + 1]
                dve.wait_ge(fin_sd, t + 1)
                link(dve.reciprocal(s_, s_))
                dve.scalar_tensor_tensor(XT2[:, t, :], XT2[:, t, :], s_, FG[:], ALU.mult, ALU.mult)\
                   .then_inc(fin_ready, 1)

        @block.tensor
        def _(pe):
            def mm(out_, lhsT, rhs, start, stop):
                return pe.matmul(out_, lhsT, rhs, start=start, stop=stop, skip_group_check=True)

            def split_mm(out_, lh, ll, rh, rl, start, stop):
                mm(out_, lh, rh, start, False)
                mm(out_, lh, rl, False, False)
                return mm(out_, ll, rh, False, stop)

            def unit(n, i=0):
                pe.wait_ge(hi_done, n + 1 + i)
                pe.wait_ge(lo_done, n + 1 + i)

            def cm_unit(n, bank, mh, ml, i=0, ready=None):
                unit(n, i)
                wh, wl = ring(WH, n), ring(WL, n)
                for k in range(KD):
                    if ready:
                        ready(k)
                    last = split_mm(PS[:, bank, :], wh[:, k, :], wl[:, k, :], mh[:, k, :], ml[:, k, :],
                                    k == 0, k == KD - 1)
                last.then_inc(unit_done, 1)

            def quad_unit(n, half, bank0, mh, ml, nk, i=0):
                unit(n, i)
                wh, wl = ring(WH, n), ring(WL, n)
                for m in range(4):
                    for k in range(2):
                        kk = 2 * half + k
                        last = split_mm(PS[:, bank0 + m, :], wh[:, k, m * P:(m + 1) * P],
                                        wl[:, k, m * P:(m + 1) * P], mh[:, kk, :], ml[:, kk, :],
                                        kk == 0, kk == nk - 1)
                last.then_inc(unit_done, 1)

            def tm_unit(n, u, bank0, xh, xl, ready=None, free=None):
                unit(n)
                wh, wl = ring(WH, n), ring(WL, n)
                for t in range(TT):
                    if u == 0 and free:
                        free(t)
                    for k in range(2):
                        kk = 2 * u + k
                        if ready and t == 0:
                            ready(kk)
                        ts = slice(t * P, (t + 1) * P)
                        last = split_mm(PS[:, bank0 + t, :], xh[:, kk, ts], xl[:, kk, ts],
                                        wh[:, k, :], wl[:, k, :], kk == 0, kk == KD - 1)
                last.then_inc(unit_done, 1)

            def x_parts(e):
                def ready(k):
                    pe.wait_ge(xh_ready, KD * e + k + 1)
                    pe.wait_ge(xl_ready, KD * e + k + 1)
                return ready

            def stats(e):
                pe.wait_ge(ss_added, KD * (e + 1))
                mm(PS[:, 7, :], ONES[:], SS[:], True, True)
                for t in range(TT):
                    last = mm(PS[:, 6, t:t + 1], SS[:, t * P:(t + 1) * P], ONES[:, 0:1], True, True)
                last.then_inc(stat_done, 1)

            def tr(out_, in_):
                return pe.transpose(out_, in_, IDENT[:])

            pe.wait_ge(consts, 2)
            pe.wait_ge(vec_in, 16 * N_VEC)
            for r in range(4):
                last = tr(PS[:, 0, r * P:(r + 1) * P], ROWS[:, r, :])
            last.then_inc(vec_t, 1)
            pe.wait_ge(vec_ready, 2)
            for t in range(TT):
                pe.wait_ge(x_in[t], 16)
                for k in range(KD):
                    last = tr(PS[:, k, t * P:(t + 1) * P], XTOK[:, t, k * P:(k + 1) * P])
                    if t == TT - 1:
                        last.then_inc(xt_done, 1)
            for j in range(4):
                for u in range(4):
                    n = U_A + 4 * j + u
                    tm_unit(n, u, 4 * (j % 2), XH, XL, x_parts(0) if j == 0 else None,
                            lambda t: pe.wait_ge(drained, 4 * j + t + 1))
                    if n == 3:
                        pe.wait_ge(drained, KD)
                        stats(0)
                        pe.wait_ge(ms_ready, 2)
            packed = [(0, 0, 512), (512, 1, 384), (1024, 2, 256), (896, 3, 128)]

            def head_z(h, c0, n):
                b0 = 2 + 3 * (h % 2)
                return PS[:, b0 + c0 // 512, c0 % 512:c0 % 512 + n]

            for i in range(12):
                pe.wait_ge(drained, DR_B + i - 1 if i >= 2 else DR_A + 8 + i + 1)
                cm_unit(U_B + i, i % 2, XH, XL)
                if i == 0:
                    pe.wait_ge(drained, DR_B)
                if i < 2:
                    pe.wait_ge(qk_ready, 4 * i + 4)
                    for c in range(KW):
                        if i:
                            pe.wait_ge(qkt_ready, c + 1)
                        for t in range(TT):
                            last = tr(PS[:, 2 + c, t * P:(t + 1) * P], QK[:, i, t, c * P:(c + 1) * P])
                        last.then_inc(qkt_t, 1)
                if i == 0:
                    pe.wait_ge(sgw_in, 16)
                    for q in range(2):
                        for g in range(4):
                            last = tr(PS[:, 6 + q, g * P:(g + 1) * P], SGW[:, 4 * q + g, :])
                        last.then_inc(wt_t, 1)
                h = i - 4
                if 0 <= h < HEADS:
                    pe.wait_ge(a_ready, h + 1)
                    rows_ = slice(DH * (h % 2), DH * (h % 2) + DH)
                    for c0, j, w in packed:
                        last = mm(PS[rows_, 2 + 3 * (h % 2), SEQ - w:SEQ], VATT[:, j, h * DH:(h + 1) * DH],
                                  ABUF[:, c0:c0 + w], j == 0, j == 3)
                    last.then_inc(av_done, 1)
                h = i - 3
                if 0 <= h < HEADS:
                    pe.wait_ge(sp_ready, 3 * h + 3)
                    for c0, j, w in packed:
                        last = mm(head_z(h, c0, w), NTRI[:], SPB[:, c0:c0 + w], False, False)
                        for c1, j1, w1 in packed:
                            if j1 > j:
                                last = mm(head_z(h, c0 + w - w1, w1), NONE_[:], SPB[:, c1:c1 + w1],
                                          False, False)
                    last.then_inc(tri_done, 1)
                h = i - 2
                if 0 <= h < HEADS:
                    if h == 0:
                        pe.wait_ge(qkt_ready, 8)
                        pe.wait_ge(consts, 8)
                    elif h == 1:
                        pe.wait_ge(sg_read, 4)
                    else:
                        pe.wait_ge(att_read, h - 1)
                    rows_ = slice(DH * (h % 2), DH * (h % 2) + DH)
                    for c0, j, w in packed:
                        last = mm(head_z(h, c0, w), QKT[rows_, 1, h // 2, j * P:(j + 1) * P],
                                  QKT[rows_, 0, h // 2, SEQ - w:SEQ], j != 3, False)
                    last.then_inc(sc_done, 1)
                if i in (1, 2):
                    if i == 1:
                        pe.wait_ge(wt_ready, 2)
                        pe.wait_ge(vn_ready, TT)
                    for c in (2 * i - 2, 2 * i - 1):
                        if i == 2:
                            pe.wait_ge(sg_read, c - 1)
                        for g in (2 * c, 2 * c + 1):
                            for t in range(TT):
                                last = mm(PS[g % 2 * DH:(g % 2 + 1) * DH, 6 + c % 2, t * P:(t + 1) * P],
                                          VSG[:, t, g * DH:(g + 1) * DH], WT[:, g, :], True, True)
                        last.then_inc(sg_done, 1)

            def branch(b, i, ln):
                n0 = U_C + 12 * b
                for q in range(2):
                    for r in range(4):
                        if b == 0 and q == 0:
                            pe.wait_ge(drained, DR_C)
                        else:
                            pe.wait_ge(drained, DR_C + 16 * b + 8 * q - 8 + r + 1 + 16 * i)
                        cm_unit(n0 + 6 * q + r, r, XH, XL, 12 * i)
                        if ln and q == 0 and r == 0:
                            pe.wait_ge(c_sum, 1)
                            pe.wait_ge(drained, DR_C + 32)
                            mm(PS[:, 4, :], ONES[:], TG1[:], True, True).then_inc(c_mean, 1)
                        if ln and q == 0 and r == 2:
                            pe.wait_ge(c_ssum, KW)
                            mm(PS[:, 5, :], ONES[:], TG0[:], True, True).then_inc(c_var, 1)
                    if q == 0:
                        pe.wait_ge(bh_ready, b + 1 + i)
                        pe.wait_ge(bl_ready, b + 1 + i)
                    pe.wait_ge(drained, DR_C + 16 * b + 8 * q + 16 * i)
                    for u in range(2):
                        quad_unit(n0 + 6 * q + 4 + u, u, 4, BH, BL, KW, 12 * i)

            pe.wait_ge(att_read, HEADS)
            branch(0, 0, False)
            branch(1, 0, False)
            branch(2, 0, True)

            for m in range(KD):
                pe.wait_ge(drained, DR_D - 7 + m if m < 4 else DR_D + m - 3)

                def ready(k):
                    pe.wait_ge(mh_ready, k + 1)
                    pe.wait_ge(ml_ready, k + 1)
                cm_unit(U_D + m, m % 4, MH, ML, 0, ready if m == 0 else None)

            def up_body(f0, i, first):
                for r in range(4):
                    pe.wait_ge(drained, DR_E + 4 * f0 - 4 + r + 1 + 4 * i)
                    cm_unit(U_E + 4 * f0 + r, r, XH, XL, 4 * i, x_parts(1) if first and r == 0 else None)
                    if first and r == 0:
                        stats(1)

            up_body(0, 0, True)
            with pe.Fori(0, NF // 2 - 1) as i:
                up_body(1, i, False)

            def down_body(kk, i, start, stop):
                pe.wait_ge(fh_ready, kk + 1 + i)
                pe.wait_ge(fl_ready, kk + 1 + i)
                for half in range(2):
                    n = U_F + 2 * kk + half
                    if start:
                        pe.wait_ge(drained, DR_F)
                        pe.wait_ge(ms_ready, 4)
                    unit(n, 2 * i)
                    wh, wl = ring(WH, n), ring(WL, n)
                    for m in range(4):
                        for k in range(2):
                            last = split_mm(PS[:, 4 * half + m, :], wh[:, k, m * P:(m + 1) * P],
                                            wl[:, k, m * P:(m + 1) * P], FH[:, kk % 2, k, :],
                                            FL[:, kk % 2, k, :], start and k == 0, stop and k == 1)
                    last.then_inc(unit_done, 1)

            down_body(0, 0, True, False)
            with pe.Fori(0, (NF // 2 - 3) // 2) as i:
                down_body(1, 2 * i, False, False)
                down_body(2, 2 * i, False, False)
            down_body(NF // 2 - 2, 0, False, False)
            down_body(NF // 2 - 1, 0, False, True)

            for j in range(3):
                for u in range(4):
                    n = U_G + 4 * j + u
                    tm_unit(n, u, 0, XH, XL, x_parts(2) if j == 0 else None,
                            lambda t: pe.wait_ge(drained, DR_F + t + 1 if j == 0
                                                 else DR_G + 4 * j - 4 + t + 1))
                    if j == 0 and u == 3:
                        pe.wait_ge(drained, DR_G)
                        stats(2)
            for m in range(KD):
                pe.wait_ge(drained, DR_GA - 1 + m if m >= 2 else DR_GA)
                cm_unit(U_GA + m, m % 2, XH, XL)
                if m == 0:
                    pe.wait_ge(rope_ready, 5)
                    pe.wait_ge(drained, DR_G)
                    pe.wait_ge(ms_ready, 6)
                if m >= 2:
                    pe.wait_ge(q2t_ready, (m - 1) + max(0, m - 2 - 4))
                for t in range(TT):
                    last = tr(PS[:, 4 + m % 2, t * P:(t + 1) * P], Q2[:, t, m * P:(m + 1) * P])
                last.then_inc(rt_t, 1)
                if m >= 4:
                    if m >= 6:
                        pe.wait_ge(q2t_ready, 2 * (m - 2) - 2)
                    for t in range(TT):
                        last = tr(PS[:, 6 + m % 2, t * P:(t + 1) * P], KDUP[:, t, m - 4, :])
                    last.then_inc(rt_t, 1)
            def block_diagonal(c):
                pe.wait_ge(uc_ready, c + 1)
                if c:
                    pe.wait_ge(gate_ri, 2 * c)
                else:
                    pe.wait_ge(lruw_in, 32)
                mm(PS[:, 2, :], LRUW[:, c, :], UC[c % 2][:], True, True)
                mm(PS[:, 3, :], LRUW[:, KD + c, :], UC[c % 2][:], True, True).then_inc(bd_done, 1)

            for s in range(19):
                if s < 16:
                    pe.wait_ge(drained, DR_GR + s - 1)
                    cm_unit(U_GR + s, s % 2, XH, XL)
                if s and s % 4 == 0:
                    block_diagonal(s // 2 - 1)
                if s >= 3:
                    g, nb = divmod(s - 3, TT)
                    pe.wait_ge(pt_ready, s - 2)
                    pe.wait_ge(s2_mask, 2 * min(s, 16))
                    if s >= 17:
                        pe.wait_ge(pv_read, s - 3)
                    kbs = (0, 1) if nb else (1,)
                    for par in range(2):
                        for kb in kbs:
                            last = mm(PS[par * DH:(par + 1) * DH, 6, 0:256],
                                      V2[:, nb - 1 + kb, g * DH:(g + 1) * DH],
                                      PT[:, kb, par].rearrange("p i q -> p (i q)"),
                                      kb == kbs[0], kb == 1)
                    last.then_inc(pv_done, 1)
                if 2 <= s < 18:
                    pe.wait_ge(s2_ready, s - 1)
                    if s >= 3:
                        pe.wait_ge(pt_ready, s - 2)
                    else:
                        pe.wait_ge(q2t_ready, KD + KVH)
                    for kb in range(2):
                        for par in range(2):
                            for idx in range(2):
                                c = (2 * par + idx) * P
                                last = tr(PS[:, 4 + kb, c:c + P],
                                          S2[s % 2][:, par, idx, kb * P:(kb + 1) * P])
                    last.then_inc(pt_t, 1)
                if s < 16:
                    g, nb = divmod(s, TT)
                    if s == 0:
                        pe.wait_ge(q2t_ready, KD + KVH)
                        pe.wait_ge(consts, 13)
                    if s >= 1:
                        pe.wait_ge(s2_mask, 2 * s)
                    if s >= 3:
                        pe.wait_ge(pv_read, s - 2)
                    for par in range(2):
                        rows_ = slice(par * DH, (par + 1) * DH)
                        for idx in range(2):
                            last = mm(PS[:, 6 + par, idx * 256:idx * 256 + 256],
                                      Q2T[rows_, 2 * g + idx, nb * P:(nb + 1) * P],
                                      K2T[rows_, g, nb * P:nb * P + 256], True, True)
                    last.then_inc(qk2_done, 1)
                if s % 4 == 3 and s < 16:
                    block_diagonal(s // 2 - 1)
            def merge_body(i0, i):
                for r in range(4):
                    if i0 == 0 and r >= 2:
                        pe.wait_ge(gate_ri, 2 * KD)
                    elif i0 == 0:
                        pe.wait_ge(drained, DR_H - 1 + r)
                    else:
                        pe.wait_ge(drained, DR_H + 4 * i0 - 4 + r + 1 + 4 * i)
                    n = U_H + 4 * i0 + r
                    if r < 2:
                        cm_unit(n, r, XH, XL, 4 * i)
                    else:
                        def ready(k):
                            pe.wait_ge(bh2_ready, 2 * i0 + k + 1)
                            pe.wait_ge(bl2_ready, 2 * i0 + k + 1)
                        cm_unit(n, r, BH2, BL2, 4 * i, ready if i0 in (0, 4) and r == 2 else None)

            merge_body(0, 0)
            with pe.Fori(0, 3) as i:
                merge_body(1, i)
            merge_body(4, 0)
            with pe.Fori(0, 3) as i:
                merge_body(5, i)
            pe.wait_ge(pv_read, 16)
            for t in range(TT):
                if t >= 2:
                    pe.wait_ge(x2t_ready, t - 1)
                for k in range(KD):
                    last = tr(PS[:, 4 + 2 * (t % 2) + k // 4, k % 4 * P:(k % 4 + 1) * P],
                              X1[:, k, t * P:(t + 1) * P])
                last.then_inc(x2t_t, 1)

            def m2_parts(k):
                pe.wait_ge(m2h_ready, k + 1)
                pe.wait_ge(m2l_ready, k + 1)

            for c in range(2):
                for u in range(4):
                    tm_unit(U_O + 4 * c + u, u, 4 * c, M2H, M2L, m2_parts if c == 0 else None,
                            lambda t: pe.wait_ge(drained, DR_O) if c == 0
                            else pe.wait_ge(x2t_ready, TT))


INPUTS = ["x", "ln1_g", "w_in", "b_gate", "sg_ln_g", "sg_ln_b", "sg_w", "sg_b", "w_a_out", "cv_w",
          "cv_b", "cv_ln_g", "cv_ln_b", "w_b_out", "q_norm_g", "k_norm_g", "w_c_out", "w_out", "ln2_g",
          "w_up", "ffn_conv_w", "ffn_conv_b", "w_down", "norm_g_2", "w_in_2", "conv_w_2", "conv_b_2",
          "lru_w_a_2", "lru_b_a_2", "lru_w_x_2", "lru_b_x_2", "lru_lambda_2", "attn_sinks_2",
          "w_rnn_out_2", "w_attn_out_2", "w_o_2", "final_norm_g_2"]


def rope_table():
    import numpy as np
    pos = np.arange(SEQ, dtype=np.float32)
    freq = np.float32(ROPE_THETA) ** (-np.arange(0, ROPE_DIM, 2, dtype=np.float32)
                                      / np.float32(ROPE_DIM))
    ang = (pos[:, None] * freq[None, :]).astype(np.float32)
    return np.concatenate([np.cos(ang), np.sin(ang)], axis=1).astype(np.float32)


def kernel(**inputs):
    import numpy as np
    import concourse.bacc as bacc
    from concourse.bass_utils import run_bass_kernel_spmd

    nc = bacc.Bacc("TRN2", target_bir_lowering=False, num_devices=1)
    arrays = {f"in_{name}": np.ascontiguousarray(inputs[name]) for name in INPUTS}
    arrays["in_rope"] = rope_table()
    args = [nc.dram_tensor(name, a.shape, mybir.dt.from_np(a.dtype), kind="ExternalInput").ap()
            for name, a in arrays.items()]
    out = nc.dram_tensor("out", inputs["x"].shape, F32, kind="ExternalOutput").ap()
    program(nc, *args, out)
    result = run_bass_kernel_spmd(nc, [arrays], core_ids=[0])
    return result.results[0]["out"]
```

```python
import math
from contextlib import ExitStack

import concourse.bass as bass
from concourse import mybir

F32 = mybir.dt.float32
F32R = mybir.dt.float32r
ALU = mybir.AluOpType
ACT = mybir.ActivationFunctionType
AX = mybir.AxisListType

P = 128
SEQ = 512
TT = SEQ // P
D = 1024
KD = D // P
W = 512
KW = W // P
CHUNK = 128
CVK = 31
HEADS = 8
DH = 64
D_FF = 2816
NF = D_FF // P
FFK = 3
EPS = 1e-6
BIG = 1e30

RNN_TAPS = 4
KVH = 4
QPK = 4
ROPE_DIM = 16
ROPE_HALF = ROPE_DIM // 2
ROPE_THETA = 500000.0
LRU_C = 8.0

IN_U, IN_VSG, IN_P, IN_G, IN_Q, IN_K, IN_V, IN_GATE = (i * W for i in range(8))
IN2_U, IN2_G, IN2_Q, IN2_KV, IN2_GA, IN2_MR, IN2_MA = 0, 1024, 2048, 3072, 3584, 4608, 5632

U_A = 0
U_B = U_A + 16
U_C = U_B + 12
U_D = U_C + 36
U_E = U_D + 8
U_F = U_E + 2 * NF
U_G = U_F + NF
U_GA = U_G + 12
U_GR = U_GA + 8
U_H = U_GR + 16
U_O = U_H + 32
U_END = U_O + 8

BRANCHES = (0, 2, 1)

DR_A = KD
DR_B = DR_A + 16
DR_C = DR_B + 12
DR_D = DR_C + 48
DR_E = DR_D + KD
DR_F = DR_E + 2 * NF
DR_G = DR_F + KD
DR_GA = DR_G + 12
DR_GR = DR_GA + 8
DR_H = DR_GR + 16
DR_O = DR_H + 32

V_CVW = 0
V_QKG = V_CVW + CVK * KW
V_FW = [128, 128 + NF * 2, 256]
V_CW2 = V_FW[1] + NF * 2
V_LN1 = V_CW2 + RNN_TAPS * KD
V_FB = V_FW[2] + NF * 2
V_BG = V_FB + NF * 2
V_LN2 = V_BG + 3 * KD
V_NG2 = V_LN2 + KD
V_CVB = 384
V_CLG = V_CVB + KW
V_CLB = V_CLG + KW
V_CB2 = V_CLB + KW
V_BA = V_CB2 + KD
V_BX = V_BA + KD
V_LAM = V_BX + KD
V_END = V_LAM + KD
assert V_LN1 + KD == 256 and V_NG2 + KD == 384

S_RTOK = 0
S_SP8 = 4
S_QKS = 16
S_LN = 80
S_ATT = 140
S_FIN = 200
S_NSP8 = 220
N_VEC = 21


def unit_kind(n):
    if n < U_B or U_G <= n < U_GA or n >= U_O:
        return "T"
    if U_C <= n < U_D:
        return "M" if (n - U_C) % 6 < 4 else "T"
    if U_F <= n < U_G:
        return "F"
    return "M"


def program(nc, x, ln1_g, w_in, b_gate, sg_ln_g, sg_ln_b, sg_w, sg_b, w_a_out, cv_w, cv_b, cv_ln_g,
            cv_ln_b, w_b_out, q_norm_g, k_norm_g, w_c_out, w_out, ln2_g, w_up, ffn_conv_w,
            ffn_conv_b, w_down, norm_g_2, w_in_2, conv_w_2, conv_b_2, lru_w_a_2, lru_b_a_2,
            lru_w_x_2, lru_b_x_2, lru_lambda_2, attn_sinks_2, w_rnn_out_2, w_attn_out_2, w_o_2,
            final_norm_g_2, rope, out):
    base = (nc.sbuf_base + 31) // 32 * 32

    def at(name, shape, dt, kb):
        size = 4 * math.prod(shape[1:])
        assert base + int(kb * 1024) + size <= 229344, name
        return nc.alloc_sbuf_tensor_at(name, shape, dt, offset=base + int(kb * 1024))

    with ExitStack() as ctx:
        STAGE = at("STAGE", [P, 2, 2048], F32, 0)
        WH = at("WH", [P, 4, 1024], F32R, 16)
        WL = at("WL", [P, 4, 1024], F32R, 32)
        XH = at("XH", [P, KD, SEQ], F32R, 48)
        XL = at("XL", [P, KD, SEQ], F32R, 64)
        IDENT = at("IDENT", [P, P], F32, 80)
        NTRI = at("NTRI", [P, P], F32, 80.5)
        NONE_ = at("NONES", [P, P], F32, 81)
        ONES = at("ONES", [P, P], F32, 81.5)
        MSTR = at("MSTR", [P, 2, P], F32, 82)
        MMIN = at("MMIN", [P, 2, P], F32, 83)
        VEC = at("VEC", [P, 512], F32, 84)
        RBC = at("RBC", [P, SEQ], F32, 86)
        SGB = at("SGB", [P, KW, P], F32, 88)
        SMALL = at("SMALL", [P, 256], F32, 90)
        SS = at("SS", [P, SEQ], F32, 91)
        SQ = at("SQ", [P, SEQ], F32, 93)
        MINC = at("MINC", [P, P], F32, 95)
        SINK = at("SINK", [P, 16], F32, 95.5)
        ROPE = at("ROPE", [P, TT, 16], F32, 95.5625)
        XTOK = at("XTOK", [P, TT, D], F32, 96)
        QK = at("QK", [P, 2, TT, W], F32, 96)
        MERG = at("MERG", [P, KD, SEQ], F32, 96)
        XCM = at("XCM", [P, KD, SEQ], F32, 112)
        QKT = at("QKT", [P, 2, KW, SEQ], F32, 112)
        VATT = at("VATT", [P, TT, W], F32, 128)
        VSG = at("VSG", [P, TT, W], F32, 136)
        TG1 = at("TG1", [P, SEQ], F32, 144)
        CPAD = at("CPAD", [P, KW, 544], F32, 146)
        CACC = at("CACC", [P, KW, SEQ], F32, 155)
        UU = at("UU", [P, KW, SEQ], F32, 163)
        ATT = at("ATT", [P, KW, SEQ], F32, 171)
        SGLN = at("SGLN", [P, 2, W], F32, 171)
        ABUF = at("ABUF", [P, 1280], F32, 179)
        WT = at("WT", [P, 8, P], F32, 184)
        SGW = at("SGW", [P, 8, P], F32, 188)
        BH = at("BH", [P, KW, SEQ], F32R, 179)
        BL = at("BL", [P, KW, SEQ], F32R, 187)
        ROWS = at("ROWS", [P, 4, P], F32, 195)
        E1 = at("E1", [P, 1280], F32, 195)
        SPB = at("SPB", [P, 1280], F32, 200)
        TG0 = at("TG0", [P, SEQ], F32, 205)
        GS = at("GS", [P, 4, SEQ], F32, 195)
        TMPY = at("TMPY", [P, SEQ], F32, 203)
        X1 = at("X1", [P, KD, SEQ], F32, 112)
        MH = at("MH", [P, KD, SEQ], F32R, 128)
        ML = at("ML", [P, KD, SEQ], F32R, 144)
        GF = at("GF", [P, NF, SEQ], F32, 128)
        FH = at("FH", [P, 2, 2, SEQ], F32R, 172)
        FL = at("FL", [P, 2, 2, SEQ], F32R, 180)
        UPB = at("UPB", [P, 4, 516], F32, 188)
        YB = at("YB", [P, 4, SEQ], F32, 197)
        YA = at("YA", [P, KD, SEQ], F32, 96)
        Q2 = at("Q2", [P, TT, D], F32, 128)
        YR = at("YR", [P, KD, SEQ], F32, 128)
        KDUP = at("KDUP", [P, TT, KVH, 2 * DH], F32, 144)
        LRUW = at("LRUW", [P, 2 * KD, P], F32, 144)
        V2 = at("V2", [P, TT, 256], F32, 152)
        Q2T = at("Q2T", [P, KD, SEQ], F32, 156)
        K2T = at("K2T", [P, KVH, P + SEQ], F32, 172)
        AM = at("AM", [P, 3, P], F32, 182)
        S2 = [at("S2A", [P, 2, 2, 256], F32, 183.5), None]
        PT = at("PT", [P, 2, 2, 2, P], F32, 187.5)
        UP2 = at("UP2", [P, 2, 516], F32, 191.5)
        RT = at("RT", [P, 4, SEQ], F32, 196)
        S2[1] = at("S2B", [P, 2, 2, 256], F32, 195.625)
        RR = [at(f"RR{i}", [P, SEQ], F32, 199.625 + 2 * i) for i in range(2)]
        II = [at(f"II{i}", [P, SEQ], F32, 203.625 + 2 * i) for i in range(2)]
        UC = [at("UC0", [P, SEQ], F32, 80.5), at("UC1", [P, SEQ], F32, 88)]
        GT = at("GT", [P, 2, SEQ], F32, 91)
        BH2 = at("BH2", [P, KD, SEQ], F32R, 156)
        BL2 = at("BL2", [P, KD, SEQ], F32R, 172)
        MERG2 = at("MERG2", [P, KD, SEQ], F32, 128)
        GS2 = at("GS2", [P, 2, SEQ], F32, 144)
        FG = at("FG", [P, D], F32, 148)
        TMP2 = at("TMP2", [P, SEQ], F32, 152)
        M2H = at("M2H", [P, KD, SEQ], F32R, 96)
        M2L = at("M2L", [P, KD, SEQ], F32R, 188)
        XT2 = at("XT2", [P, TT, D], F32, 48)
        SQF = at("SQF", [P, D], F32, 64)

        PS = ctx.enter_context(nc.psum_tensor("PS", [P, 8, 512], F32))
        XSCR = nc.dram_tensor("x_channel_major", [P, KD * SEQ], F32, kind="Internal").ap()

        def sem(name):
            return ctx.enter_context(nc.semaphore(name))

        landed = [sem("landed0"), sem("landed1")]
        x_in = [sem(f"x_in{t}") for t in range(TT)]
        vec_in, bc_in, sgw_in = sem("vec_in"), sem("bc_in"), sem("sgw_in")
        xscr_out, xres_in = sem("xscr_out"), sem("xres_in")
        lruw_in, fg_in, stored = sem("lruw_in"), sem("fg_in"), sem("stored")
        consts = sem("consts")
        ss_added = sem("ss_added")
        ss_clear = sem("ss_clear")
        hi_done, lo_done = sem("hi_done"), sem("lo_done")
        unit_done = sem("unit_done")
        drained = sem("drained")
        xt_done = sem("xt_done")
        vec_t, vec_ready = sem("vec_t"), sem("vec_ready")
        wt_t, wt_ready = sem("wt_t"), sem("wt_ready")
        xh_ready, xl_ready, sq_ready = sem("xh_ready"), sem("xl_ready"), sem("sq_ready")
        stat_done, ms_ready, rt_ready, r_ready = (sem("stat_done"), sem("ms_ready"),
                                                  sem("rt_ready"), sem("r_ready"))
        qk_sq, qk_red, qk_ms, qk_rt, qk_ready = (sem("qk_sq"), sem("qk_red"), sem("qk_ms"),
                                                 sem("qk_rt"), sem("qk_ready"))
        qkt_t, qkt_ready = sem("qkt_t"), sem("qkt_ready")
        vg_ready, vg_var, vg_sd, vn_ready = (sem("vg_ready"), sem("vg_var"), sem("vg_sd"),
                                             sem("vn_ready"))
        sg_done, sg_read = sem("sg_done"), sem("sg_read")
        sc_done, ln_ready, sp_ready, tri_done = (sem("sc_done"), sem("ln_ready"), sem("sp_ready"),
                                                 sem("tri_done"))
        min_ready, a_ready, av_done, att_read = (sem("min_ready"), sem("a_ready"), sem("av_done"),
                                                 sem("att_read"))
        tg_act, tg_used = sem("tg_act"), sem("tg_used")
        c_sum, c_mean, c_cent, c_sq, c_ssum, c_var, c_ve, c_sd, c_norm, c_ready = (
            sem("c_sum"), sem("c_mean"), sem("c_cent"), sem("c_sq"), sem("c_ssum"), sem("c_var"),
            sem("c_ve"), sem("c_sd"), sem("c_norm"), sem("c_ready"))
        bh_ready, bl_ready = sem("bh_ready"), sem("bl_ready")
        gs_ready, merged = sem("gs_ready"), sem("merged")
        mh_ready, ml_ready = sem("mh_ready"), sem("ml_ready")
        y_first, y_silu, gf_ready = sem("y_first"), sem("y_silu"), sem("gf_ready")
        y_conv = sem("y_conv")
        fh_ready, fl_ready = sem("fh_ready"), sem("fl_ready")
        rope_ready, rt_t, q2t_ready = sem("rope_ready"), sem("rt_t"), sem("q2t_ready")
        ya_silu = sem("ya_silu")
        uc_first, uc_ready, bd_done = sem("uc_first"), sem("uc_ready"), sem("bd_done")
        gate_ri, tanh_ready, a_exp, a_sq = sem("gate_ri"), sem("tanh_ready"), sem("a_exp"), sem("a_sq")
        bsq_ready, bsqrt, iu_ready, h_ready = (sem("bsq_ready"), sem("bsqrt"), sem("iu_ready"),
                                               sem("h_ready"))
        yr_ready, yg_sig, yg_ready = sem("yr_ready"), sem("yg_sig"), sem("yg_ready")
        s2_mask, qk2_done, s2_max, s2_exp, s2_ready, pt_t, pt_ready, pv_done, pv_read = (
            sem("s2_mask"), sem("qk2_done"), sem("s2_max"), sem("s2_exp"), sem("s2_ready"),
            sem("pt_t"), sem("pt_ready"), sem("pv_done"), sem("pv_read"))
        c_tap, y_tap = sem("c_tap"), sem("y_tap")
        bh2_ready, bl2_ready, gs2_ready, merged2 = (sem("bh2_ready"), sem("bl2_ready"),
                                                    sem("gs2_ready"), sem("merged2"))
        m2h_ready, m2l_ready = sem("m2h_ready"), sem("m2l_ready")
        x2t_t, x2t_ready, fin_sq, fin_ms, fin_sd, fin_ready = (
            sem("x2t_t"), sem("x2t_ready"), sem("fin_sq"), sem("fin_ms"), sem("fin_sd"),
            sem("fin_ready"))
        vchain, schain, gchain = sem("vchain"), sem("schain"), sem("gchain")

        def staged(n):
            kind, st, u = unit_kind(n), STAGE[:, n // 2 % 2, :], n % 2
            if kind == "M":
                return st.rearrange("p (k c) -> p k c", k=8)[:, :, u * P:(u + 1) * P]
            if kind == "T":
                return st[:, u * 1024:(u + 1) * 1024].rearrange("p (k c) -> p k c", k=2)
            return st.rearrange("p (k c) -> p k c", k=2)[:, :, u * 512:(u + 1) * 512]

        def ring(buf, n):
            k = 8 if unit_kind(n) == "M" else 2
            return buf[:, n % 4, :].rearrange("p (k c) -> p k c", k=k)

        def col(c, n=1):
            return VEC[:, c:c + n]

        def rows(w, r0, nr, c0, ncol):
            return w[0, r0 * P:(r0 + nr) * P, c0:c0 + ncol].rearrange("(k p) c -> p k c", p=P)

        def transfers():
            for c0 in (IN_Q, IN_K, IN_VSG, IN_V):
                for r0 in (0, 4):
                    yield rows(w_in, r0, 4, c0, 512)
            for c0 in (IN_P, IN_G, IN_P + 256, IN_G + 256, IN_U, IN_U + 256):
                yield rows(w_in, 0, 8, c0, 256)
            for b in BRANCHES:
                for quad in range(2):
                    for h in range(2):
                        yield rows(w_in, 0, 8, IN_GATE + b * D + quad * 512 + h * 256, 256)
                    yield rows((w_a_out, w_b_out, w_c_out)[b], 0, 4, quad * 512, 512)
            for m in range(4):
                yield rows(w_out, 0, 8, m * 256, 256)
            for f in range(NF // 2):
                yield rows(w_up, 0, 8, f * 256, 256)
                yield rows(w_up, 0, 8, D_FF + f * 256, 256)
            for kk in range(NF // 2):
                yield rows(w_down, 2 * kk, 2, 0, 1024)
            for c0 in (IN2_Q, IN2_Q + 512, IN2_KV):
                for r0 in (0, 4):
                    yield rows(w_in_2, r0, 4, c0, 512)
            for m in range(4):
                yield rows(w_in_2, 0, 8, IN2_GA + m * 256, 256)
            for m in range(4):
                yield rows(w_in_2, 0, 8, IN2_U + m * 256, 256)
                yield rows(w_in_2, 0, 8, IN2_G + m * 256, 256)
            for c0, w in ((IN2_MR, w_rnn_out_2), (IN2_MA, w_attn_out_2)):
                for m in range(4):
                    yield rows(w_in_2, 0, 8, c0 + m * 256, 256)
                    yield rows(w, 0, 8, m * 256, 256)
            for c in range(2):
                for r0 in (0, 4):
                    yield rows(w_o_2, r0, 4, c * 512, 512)

        block = ctx.enter_context(nc.Block())

        @block.sync
        def _(sp):
            xt = x.rearrange("o (t p) d -> p (o t) d", p=P)
            for t in range(TT):
                sp.dma_start(XTOK[:, t, :], xt[:, t, :]).then_inc(x_in[t], 16)
            for p, src in enumerate(transfers()):
                kd, ncol = src.shape[1], src.shape[2]
                if p >= 2:
                    sp.wait_ge(lo_done, 2 * p - 2)
                sp.dma_start(STAGE[:, p % 2, :].rearrange("p (k c) -> p k c", k=kd, c=ncol), src)\
                  .then_inc(landed[p % 2], 16)
                if p == 2:
                    sp.dma_start(SGW[:], sg_w[0].rearrange("g t s -> t g s")).then_inc(sgw_in, 16)
                    sp.dma_start(SGLN[:, 0, :], sg_ln_g[0].partition_broadcast(P)).then_inc(bc_in, 16)
                    sp.dma_start(SGLN[:, 1, :], sg_ln_b[0].partition_broadcast(P)).then_inc(bc_in, 16)
                    for g in range(8):
                        sp.dma_start(SGB[g % 2 * DH:(g % 2 + 1) * DH, g // 2, :],
                                      sg_b[0, g].partition_broadcast(DH)).then_inc(bc_in, 16)
                    sp.dma_start(SINK[:], attn_sinks_2[0].partition_broadcast(P)).then_inc(bc_in, 16)
                    sp.dma_start(ROPE[:], rope.rearrange("(t p) c -> p t c", p=P)).then_inc(bc_in, 16)
                if p == 3:
                    sp.wait_ge(drained, KD)
                    sp.dma_start(XSCR, XCM[:].rearrange("p k s -> p (k s)")).then_inc(xscr_out, 16)
                if p == U_C // 2 + 6:
                    sp.wait_ge(xscr_out, 16)
                    sp.wait_ge(sc_done, HEADS)
                    sp.dma_start(X1[:].rearrange("p k s -> p (k s)"), XSCR).then_inc(xres_in, 16)
                if p == U_GR // 2 + 1:
                    sp.wait_ge(q2t_ready, KD + KVH)
                    sp.dma_start(LRUW[:, 0:KD, :], lru_w_a_2[0].rearrange("n c d -> c n d"))\
                      .then_inc(lruw_in, 16)
                    sp.dma_start(LRUW[:, KD:, :], lru_w_x_2[0].rearrange("n c d -> c n d"))\
                      .then_inc(lruw_in, 16)
                if p == U_H // 2 + 2:
                    sp.wait_ge(bd_done, KD)
                    sp.dma_start(FG[:], final_norm_g_2.partition_broadcast(P)).then_inc(fg_in, 16)
            for t in range(TT):
                sp.wait_ge(fin_ready, t + 1)
                sp.dma_start(out.rearrange("o (t p) d -> p (o t) d", p=P)[:, t, :], XT2[:, t, :])\
                  .then_inc(stored, 16)
            sp.wait_ge(stored, 16 * TT)

        @block.gpsimd
        def _(pool):
            n = 0

            def mask(t, fill, in_value, pattern, base, mult, op):
                nonlocal n
                pool.memset(t, in_value).then_inc(gchain, 1)
                n += 1
                pool.wait_ge(gchain, n)
                pool.affine_select(out=t, in_=t, compare_op=op, fill=fill, base=base,
                                   pattern=pattern, channel_multiplier=mult).then_inc(consts, 1)

            mask(IDENT[:], 0.0, 1.0, [[-1, P]], 0, 1, ALU.is_equal)
            pool.memset(ONES[:], 1.0).then_inc(consts, 1)
            pool.memset(SS[:], 0.0).then_inc(ss_clear, 1)
            mask(MINC[:], 0.0, 1.0, [[1, P]], 0, -1, ALU.is_ge)
            mask(NTRI[:], 0.0, -1.0, [[-1, P]], 0, 1, ALU.is_ge)
            pool.memset(NONE_[:], -1.0).then_inc(consts, 1)
            mask(MSTR[:], 0.0, 1.0, [[0, 2], [1, P]], 0, -1, ALU.is_gt)
            mask(MMIN[:], -BIG, BIG, [[0, 2], [1, P]], 0, -1, ALU.is_gt)
            pool.memset(CPAD[:, :, 0:32], 0.0).then_inc(consts, 1)

            def squares(e):
                for k in range(KD):
                    pool.wait_ge(sq_ready, KD * e + k + 1)
                    if k == 0:
                        pool.wait_ge(ss_clear, e + 1)
                    else:
                        pool.wait_ge(ss_added, KD * e + k)
                    pool.tensor_tensor(SS[:], SS[:], SQ[:], ALU.add).then_inc(ss_added, 1)
                if e < 2:
                    pool.wait_ge(stat_done, e + 1)
                    pool.memset(SS[:], 0.0).then_inc(ss_clear, 1)

            squares(0)
            squares(1)
            pool.wait_ge(merged, KD)
            pool.memset(UPB[:, :, 0:4], 0.0).then_inc(consts, 1)
            squares(2)
            pool.wait_ge(unit_done, U_G)
            pool.memset(AM[:, 0, :], -BIG).then_inc(gchain, 1)
            pool.memset(AM[:, 1:3, :], 0.0).then_inc(gchain, 1)
            n += 2
            pool.wait_ge(gchain, n)
            pool.affine_select(out=AM[:, 1, :], in_=AM[:, 1, :], compare_op=ALU.is_gt, fill=-BIG,
                               base=0, pattern=[[1, P]], channel_multiplier=-1).then_inc(consts, 1)
            pool.affine_select(out=AM[:, 2, :], in_=AM[:, 2, :], compare_op=ALU.is_ge, fill=-BIG,
                               base=0, pattern=[[-1, P]], channel_multiplier=1).then_inc(consts, 1)
            pool.memset(K2T[:, :, 0:P], 0.0).then_inc(consts, 1)
            pool.memset(UP2[:, :, 0:4], 0.0).then_inc(consts, 1)
            for m in range(KD // 2):
                pool.wait_ge(yg_sig, 2 * m + 2)
                pool.tensor_tensor(GT[:], GT[:], UP2[:, :, 4:516], ALU.mult).then_inc(yg_ready, 1)
                for c in (2 * m, 2 * m + 1):
                    pool.wait_ge(gate_ri, 2 * c + 2)
                    pool.tensor_tensor(II[c % 2][:], II[c % 2][:], UC[c % 2][:], ALU.mult)\
                        .then_inc(iu_ready, 1)
                for c in (2 * m, 2 * m + 1):
                    pool.wait_ge(a_exp, c + 1)
                    pool.wait_ge(iu_ready, c + 1)
                    pool.tensor_tensor(UC[c % 2][:], YR[:, c, :], YR[:, c, :], ALU.mult)\
                        .then_inc(a_sq, 1)
                pool.wait_ge(yg_ready, m + 1)
                for c in (2 * m, 2 * m + 1):
                    pool.wait_ge(h_ready, c + 1)
                    pool.tensor_tensor(YR[:, c, :], YR[:, c, :], GT[:, c % 2, :], ALU.mult)\
                        .then_inc(yr_ready, 1)

        @block.scalar
        def _(act):
            def vec_rows(c, src):
                n, r = src.shape[0], c
                assert r // P == (r + n - 1) // P
                act.dma_start(ROWS[r % P:r % P + n, r // P, :], src).then_inc(vec_in, 16)

            def r128(v):
                return v.rearrange("(n p) -> n p", p=P)

            def dma_vectors():
                vec_rows(V_LN1, r128(ln1_g[0]))
                for j in range(2):
                    vec_rows(V_FW[j], r128(ffn_conv_w[0, j]))
                vec_rows(V_CW2, conv_w_2[0].rearrange("j (n p) -> (j n) p", p=P))
                vec_rows(V_CVW, cv_w[0].rearrange("j (n p) -> (j n) p", p=P))
                for i, g in enumerate((q_norm_g, k_norm_g)):
                    for h in range(2):
                        act.dma_start(ROWS[V_QKG + i:V_QKG + i + 1, 0, h * DH:(h + 1) * DH], g)\
                           .then_inc(vec_in, 16)
                vec_rows(V_FW[2], r128(ffn_conv_w[0, 2]))
                vec_rows(V_FB, r128(ffn_conv_b[0]))
                vec_rows(V_BG, b_gate[0].rearrange("j (n p) -> (j n) p", p=P))
                vec_rows(V_LN2, r128(ln2_g[0]))
                vec_rows(V_NG2, r128(norm_g_2[0]))
                for c, v in ((V_CVB, cv_b), (V_CLG, cv_ln_g), (V_CLB, cv_ln_b), (V_CB2, conv_b_2),
                             (V_BA, lru_b_a_2), (V_BX, lru_b_x_2), (V_LAM, lru_lambda_2)):
                    vec_rows(c, r128(v[0]))
                return 21

            act.wait_ge(vec_ready, 1)
            assert dma_vectors() == N_VEC

            ns = 0

            def link(ins):
                nonlocal ns
                ins.then_inc(schain, 1)
                ns += 1
                act.wait_ge(schain, ns)

            def hi(n, i=0):
                act.wait_ge(landed[n // 2 % 2], 16 * (n // 4 + 1) + 16 * i)
                if n >= 4:
                    act.wait_ge(unit_done, n - 3 + 4 * i)
                act.activation(ring(WH, n), staged(n), ACT.Copy).then_inc(hi_done, 1)

            def feed(e, k, src, g, dr):
                act.wait_ge(drained, dr)
                act.activation(XH[:, k, :], src[:, k, :], ACT.Copy, scale=col(g + k))\
                   .then_inc(xh_ready, 1)
                if KD * e + k > 0:
                    act.wait_ge(ss_added, KD * e + k)
                act.activation(SQ[:], src[:, k, :], ACT.Square).then_inc(sq_ready, 1)

            def roots(e):
                act.wait_ge(ms_ready, 2 * e + 1)
                act.activation(RBC[:], RBC[:], ACT.Sqrt).then_inc(rt_ready, 1)
                act.wait_ge(ms_ready, 2 * e + 2)
                act.activation(SMALL[:, 0:TT], SMALL[:, 0:TT], ACT.Sqrt).then_inc(rt_ready, 1)

            hi(0)
            hi(1)
            act.wait_ge(vec_ready, 2)
            for k in range(KD):
                feed(0, k, XCM, V_LN1, k + 1)
                if k in (1, 3):
                    hi(2 + k // 2)
            for n in range(U_A, U_B):
                hi(n + 4)
                if n == 2:
                    roots(0)
                j, t = divmod(n - 4, 4)
                if j in (0, 1):
                    act.wait_ge(drained, DR_A + 4 * j + t + 1)
                    if 4 * j + t > 0:
                        act.wait_ge(qk_red, 4 * j + t)
                    act.activation(TG1[:], QK[:, j, t, :], ACT.Square).then_inc(qk_sq, 1)
                if n == U_B - 4:
                    act.wait_ge(qk_ms, 1)
                    act.activation(SMALL[:, S_QKS:S_QKS + 64], SMALL[:, S_QKS:S_QKS + 64], ACT.Sqrt)\
                       .then_inc(qk_rt, 1)
                if j == 2:
                    act.wait_ge(drained, DR_A + 8 + t + 1)
                    act.activation(VSG[:, t, :], VSG[:, t, :], ACT.Gelu_apprx_tanh)\
                       .then_inc(vg_ready, 1)
            act.wait_ge(vg_var, 1)
            act.activation(SMALL[:, S_LN + 40:S_LN + 44], SMALL[:, S_LN + 40:S_LN + 44], ACT.Sqrt)\
               .then_inc(vg_sd, 1)
            for i in range(12):
                hi(U_B + i + 4)
                if i in (0, 1):
                    if i == 0:
                        act.wait_ge(xscr_out, 16)
                        act.wait_ge(vec_ready, 3)
                    for c in range(KW):
                        act.wait_ge(qkt_t, 4 * i + c + 1)
                        act.activation(QKT[:, i, c, :], PS[:, 2 + c, :], ACT.Copy,
                                       scale=col(V_QKG + i)).then_inc(qkt_ready, 1)
                h = i - 3
                if 0 <= h < HEADS:
                    b0 = 2 + 3 * (h % 2)
                    act.wait_ge(min_ready, 2 * h + 2)
                    if h > 0:
                        act.wait_ge(av_done, h)
                    act.activation(ABUF[:], PS[:, b0:b0 + 3, :].rearrange("p b c -> p (b c)")[:, 0:1280],
                                   ACT.Exp).then_inc(a_ready, 1)
                h = i - 2
                if 0 <= h < HEADS:
                    b0 = 2 + 3 * (h % 2)
                    act.wait_ge(sc_done, h + 1)
                    if h > 0:
                        act.wait_ge(sp_ready, 3 * h)
                    link(act.activation(E1[:], PS[:, b0:b0 + 3, :].rearrange("p b c -> p (b c)")[:, 0:1280],
                                        ACT.Abs))
                    link(act.activation(E1[:], E1[:], ACT.Exp, scale=-1.0))
                    act.activation(E1[:], E1[:], ACT.Ln, bias=1.0).then_inc(ln_ready, 1)
                if i in (2, 3, 6, 7, 8, 9, 10, 11):
                    act.wait_ge(drained, DR_B + i + 1)
                    t = (TG0, TG1)[i % 2]
                    act.activation(t[:], t[:], ACT.Sigmoid if i < 8 else ACT.Gelu_apprx_tanh)\
                       .then_inc(tg_act, 1)
            for b in range(3):
                if b == 0:
                    act.wait_ge(tg_used, 8)
                    act.wait_ge(av_done, HEADS)
                    src = UU
                elif b == 1:
                    act.wait_ge(att_read, HEADS)
                    src = ATT
                for q in range(2):
                    for r in range(6):
                        n = U_C + 12 * b + 6 * q + r
                        hi(n + 4)
                        if b < 2 and q == 0 and r == 0:
                            if b:
                                act.wait_ge(unit_done, n)
                            act.activation(BH[:], src[:], ACT.Copy).then_inc(bh_ready, 1)
                        if b == 1 and q == 1 and r == 3:
                            for c in range(KW):
                                act.wait_ge(c_cent, c + 1)
                                if c:
                                    act.wait_ge(c_ssum, c)
                                act.activation(TG1[:], CACC[:, c, :], ACT.Square).then_inc(c_sq, 1)
                        if r < 4:
                            act.wait_ge(drained, DR_C + 16 * b + 8 * q + r + 1)
                            act.activation(GS[:, r, :], GS[:, r, :], ACT.Sigmoid,
                                           bias=col(V_BG + BRANCHES[b] * KD + 4 * q + r))\
                               .then_inc(gs_ready, 1)
                        if b == 2 and q == 0 and r == 0:
                            act.wait_ge(unit_done, U_C + 24)
                            act.wait_ge(c_ve, 1)
                            act.activation(TG0[:], TG0[:], ACT.Sqrt).then_inc(c_sd, 1)
                            for c in range(KW):
                                act.wait_ge(c_norm, c + 1)
                                act.activation(CACC[:, c, :], CACC[:, c, :], ACT.Silu,
                                               scale=col(V_CLG + c), bias=col(V_CLB + c))\
                                   .then_inc(c_ready, 1)
                            act.wait_ge(c_ready, KW)
                            act.activation(BH[:], CACC[:], ACT.Copy).then_inc(bh_ready, 1)
                    if b == 2 and q == 0:
                        for m in range(4):
                            act.wait_ge(merged, m + 1)
                            act.activation(MH[:, m, :], MERG[:, m, :], ACT.Copy).then_inc(mh_ready, 1)
            for m in range(4, KD):
                act.wait_ge(merged, m + 1)
                act.activation(MH[:, m, :], MERG[:, m, :], ACT.Copy).then_inc(mh_ready, 1)
            for m in range(KD):
                hi(U_D + m + 4)
                feed(1, m, X1, V_LN2, DR_D + m + 1)
            roots(1)

            def up_body(i, f0, last):
                f = f0 + i
                n = U_E + 4 * f0
                for r in range(4):
                    if last:
                        hi(n + 4 + r)
                    else:
                        hi(U_E + 4 + r + 4 * f0, i)
                    act.wait_ge(drained, DR_E + 4 * f + r + 1)
                    if f0 > 0:
                        act.wait_ge(gf_ready, 2 * f - 1 + r % 2)
                    c = r % 2 + (NF if r >= 2 else 0) + 2 * f
                    act.activation(YB[:, r, :], UPB[:, r, 4:516], ACT.Identity,
                                   scale=VEC[:, bass.ds(V_FW[2] + c, 1)],
                                   bias=VEC[:, bass.ds(V_FB + c, 1)]).then_inc(y_first, 1)
                    if r >= 2:
                        act.wait_ge(y_conv, 4 * f + r - 1)
                        act.activation(YB[:, r - 2, :], YB[:, r - 2, :], ACT.Silu)\
                           .then_inc(y_silu, 1)

            act.wait_ge(consts, 9)
            up_body(0, 0, False)
            with act.Fori(0, NF // 2 - 2) as i:
                up_body(i, 1, False)

            def ff_hi(kk, i=0):
                if kk >= 2:
                    act.wait_ge(unit_done, U_F + 2 * kk - 2 + 4 * i)
                act.wait_ge(gf_ready, 2 * kk + 2 + 4 * i)
                act.activation(FH[:, kk % 2], GF[:, bass.ds(2 * kk + 4 * i, 2), :], ACT.Copy)\
                   .then_inc(fh_ready, 1)

            def down_body(kk, i=0, more=True):
                if more:
                    ff_hi(kk + 1, i)
                hi(U_F + 2 * kk + 4, i)
                hi(U_F + 2 * kk + 5, i)

            ff_hi(0)
            up_body(0, NF // 2 - 1, True)
            down_body(0)
            with act.Fori(0, (NF // 2 - 3) // 2) as i:
                down_body(1, i)
                down_body(2, i)
            down_body(NF // 2 - 2)
            down_body(NF // 2 - 1, more=False)
            for m in range(KD):
                feed(2, m, X1, V_NG2, DR_F + m + 1)
            lam = SMALL[:, S_SP8:S_SP8 + KD]
            link(act.activation(lam, col(V_LAM, KD), ACT.Exp, scale=-1.0))
            link(act.activation(lam, lam, ACT.Ln, bias=1.0))
            act.activation(SMALL[:, S_NSP8:S_NSP8 + KD], lam, ACT.Copy, scale=-LRU_C)
            link(act.activation(lam, lam, ACT.Copy, scale=LRU_C))
            for i in range(12):
                hi(U_G + i + 4)
                if i == 2:
                    roots(2)
            for m in range(KD):
                hi(U_GA + m + 4)
                act.wait_ge(rt_t, m + 1 + max(0, m - 4))
                act.activation(Q2T[:, m, :], PS[:, 4 + m % 2, :], ACT.Copy).then_inc(q2t_ready, 1)
                if m >= 4:
                    act.wait_ge(rt_t, 2 * m - 2)
                    act.activation(K2T[:, m - 4, P:], PS[:, 6 + m % 2, :], ACT.Copy)\
                       .then_inc(q2t_ready, 1)
                act.wait_ge(drained, DR_GA + m + 1)
                act.activation(YA[:, m, :], YA[:, m, :], ACT.Silu).then_inc(ya_silu, 1)

            def window_exp(s):
                buf, c0 = S2[s % 2], S_ATT + 20 * (s % 2)
                act.wait_ge(s2_max, s + 1)
                for par in range(2):
                    for idx in range(2):
                        j = 2 * par + idx
                        act.activation(buf[:, par, idx, :], buf[:, par, idx, :], ACT.Exp,
                                       bias=SMALL[:, c0 + 4 + j:c0 + 5 + j],
                                       accum_out=SMALL[:, c0 + 12 + j:c0 + 13 + j])\
                           .then_inc(s2_exp, 1)
                act.activation(SMALL[:, c0 + 8:c0 + 12], SMALL[:, c0 + 8:c0 + 12],
                               ACT.Exp).then_inc(s2_exp, 1)

            def window_pt(s):
                act.wait_ge(pt_t, s + 1)
                if s > 0:
                    act.wait_ge(pv_done, s)
                act.activation(PT[:].rearrange("p a b c d -> p (a b c d)"),
                               PS[:, 4:6, :].rearrange("p b c -> p (b c)"), ACT.Copy)\
                   .then_inc(pt_ready, 1)

            def first_tap(c):
                act.wait_ge(drained, DR_GR + 4 * (c // 2) + c % 2 + 1)
                if c >= 2:
                    act.wait_ge(iu_ready, c - 1)
                    act.wait_ge(bsq_ready, c - 1)
                act.activation(UC[c % 2][:], UP2[:, c % 2, 4:516], ACT.Identity,
                               scale=col(V_CW2 + 3 * KD + c), bias=col(V_CB2 + c))\
                   .then_inc(uc_first, 1)

            def rec_sigmoid(c):
                act.wait_ge(bd_done, c + 1)
                if c >= 2:
                    act.wait_ge(h_ready, c - 1)
                act.activation(RR[c % 2][:], PS[:, 2, :], ACT.Sigmoid, bias=col(V_BA + c))\
                   .then_inc(gate_ri, 1)
                act.activation(II[c % 2][:], PS[:, 3, :], ACT.Sigmoid, bias=col(V_BX + c))\
                   .then_inc(gate_ri, 1)

            def rec_exp(c):
                act.wait_ge(gate_ri, 2 * c + 2)
                act.activation(YR[:, c, :], RR[c % 2][:], ACT.Exp,
                               scale=SMALL[:, S_NSP8 + c:S_NSP8 + c + 1]).then_inc(a_exp, 1)
                act.activation(RR[c % 2][:], RR[c % 2][:], ACT.Tanh,
                               scale=SMALL[:, S_SP8 + c:S_SP8 + c + 1]).then_inc(tanh_ready, 1)

            def rec_root(c):
                act.wait_ge(bsq_ready, c + 1)
                act.activation(RR[c % 2][:], RR[c % 2][:], ACT.Sqrt).then_inc(bsqrt, 1)

            def rnn_hi(ks):
                for k in ks:
                    act.wait_ge(yr_ready, k + 1)
                    act.activation(BH2[:, k, :], YR[:, k, :], ACT.Copy).then_inc(bh2_ready, 1)

            act.wait_ge(consts, 13)
            for s in range(16 + 3):
                m, q = divmod(s, 4)
                if s < 16:
                    hi(U_GR + s + 4)
                if 2 <= s < 18:
                    window_pt(s - 2)
                if q == 0 and m:
                    rec_sigmoid(2 * m - 1)
                if q == 2 and s < 16:
                    first_tap(2 * m + 1)
                if s < 16:
                    window_exp(s)
                if q == 0 and m:
                    rec_exp(2 * m - 2)
                    rec_exp(2 * m - 1)
                if q == 1 and s < 16:
                    first_tap(2 * m)
                if q == 1 and m:
                    rec_root(2 * m - 2)
                    rec_root(2 * m - 1)
                if s == 17:
                    act.wait_ge(qk2_done, 16)
                    rnn_hi(range(5))
                if q == 3 and s < 16:
                    rec_sigmoid(2 * m)
                    for c in (2 * m, 2 * m + 1):
                        act.wait_ge(drained, DR_GR + 4 * m + 2 + c % 2 + 1)
                        if c % 2 == 0:
                            act.wait_ge(uc_ready, 2 * m + 2)
                        act.activation(UP2[:, c % 2, 4:516], GT[:, c % 2, :], ACT.Sigmoid)\
                           .then_inc(yg_sig, 1)
            def merge_body(i0, i=0):
                for r in range(4):
                    hi(U_H + 4 * i0 + r + 4, i)
                    if r < 2:
                        act.wait_ge(drained, DR_H + 4 * i0 + r + 1 + 4 * i)
                        act.activation(GS2[:, r, :], GS2[:, r, :], ACT.Sigmoid).then_inc(gs2_ready, 1)
                if i0 >= 4:
                    for m in (2 * i0 - 8, 2 * i0 - 7):
                        act.wait_ge(merged2, m + 1 + 2 * i)
                        act.activation(M2H[:, bass.ds(m + 2 * i, 1), :], MERG2[:, bass.ds(m + 2 * i, 1), :],
                                       ACT.Copy).then_inc(m2h_ready, 1)

            rnn_hi(range(5, KD))
            merge_body(0)
            with act.Fori(0, 3) as i:
                merge_body(1, i)
            act.wait_ge(unit_done, U_H + 16)
            act.wait_ge(pv_read, 16)
            for k in range(KD):
                act.activation(BH2[:, k, :], YA[:, k, :], ACT.Copy).then_inc(bh2_ready, 1)
            merge_body(4)
            with act.Fori(0, 2) as i:
                merge_body(5, i)
            merge_body(7)
            for t in range(TT):
                act.wait_ge(x2t_t, t + 1)
                act.activation(XT2[:, t, :], PS[:, 4 + 2 * (t % 2):6 + 2 * (t % 2), :]
                               .rearrange("p b c -> p (b c)"), ACT.Copy).then_inc(x2t_ready, 1)
            for i in range(4):
                hi(U_O + i + 4)
            for t in range(TT):
                act.wait_ge(drained, DR_O + 4 + t + 1)
                if t:
                    act.wait_ge(fin_sq, t)
                act.activation(SQF[:], XT2[:, t, :], ACT.Square,
                               accum_out=SMALL[:, S_FIN + t:S_FIN + t + 1]).then_inc(fin_sq, 1)
            for t in range(TT):
                act.wait_ge(fin_ms, t + 1)
                act.activation(SMALL[:, S_FIN + t:S_FIN + t + 1], SMALL[:, S_FIN + t:S_FIN + t + 1],
                               ACT.Sqrt).then_inc(fin_sd, 1)

        @block.vector
        def _(dve):
            nv = 0

            def link(ins):
                nonlocal nv
                ins.then_inc(vchain, 1)
                nv += 1
                dve.wait_ge(vchain, nv)

            def lo(n, i=0):
                dve.wait_ge(hi_done, n + 1 + 4 * i)
                dve.tensor_tensor(ring(WL, n), staged(n), ring(WH, n).bitcast(F32), ALU.subtract)\
                   .then_inc(lo_done, 1)

            def feed(e, k, src, g):
                dve.wait_ge(xh_ready, KD * e + k + 1)
                dve.scalar_tensor_tensor(XL[:, k, :], src[:, k, :], col(g + k),
                                         XH[:, k, :].bitcast(F32), ALU.mult, ALU.subtract)\
                   .then_inc(xl_ready, 1)

            def norm(e):
                dve.wait_ge(stat_done, e + 1)
                b = 2 if e == 2 else 6
                dve.tensor_scalar(RBC[:], PS[:, b + 1, :], 1.0 / D, EPS, ALU.mult, ALU.add)\
                   .then_inc(ms_ready, 1)
                dve.tensor_scalar(SMALL[:, 0:TT], PS[:, b, 0:TT], 1.0 / D, EPS, ALU.mult, ALU.add)\
                   .then_inc(ms_ready, 1)
                dve.wait_ge(rt_ready, 2 * e + 2)
                dve.reciprocal(SMALL[:, 0:TT], SMALL[:, 0:TT]).then_inc(r_ready, 1)
                dve.reciprocal(RBC[:], RBC[:]).then_inc(r_ready, 1)

            def rtok(t):
                return SMALL[:, t:t + 1]

            dve.memset(ROWS[:], 0.0).then_inc(vec_ready, 1)
            for k in range(KD):
                dve.wait_ge(xt_done, k + 1)
                dve.tensor_copy(XCM[:, k, :], PS[:, k, :]).then_inc(drained, 1)
            dve.wait_ge(drained, KD)
            dve.wait_ge(vec_t, 1)
            dve.tensor_copy(VEC[:], PS[:, 0, :]).then_inc(vec_ready, 1)
            dve.wait_ge(vec_ready, 2)
            dve.tensor_scalar(col(V_QKG), col(V_QKG), DH ** -0.5, None, ALU.mult)\
               .then_inc(vec_ready, 1)
            for k in range(KD):
                feed(0, k, XCM, V_LN1)
                if k in (1, 3):
                    lo(k - 1)
                    lo(k)
            ssq = SMALL[:, S_QKS:S_QKS + 64]
            for n in range(U_A, U_B + 4):
                j, t = divmod(n - 4, 4)
                if n < U_B:
                    lo(n + 4)
                if n == 2:
                    norm(0)
                    dve.wait_ge(r_ready, 2)
                if n >= 4:
                    if t == 0:
                        dve.wait_ge(unit_done, U_A + 4 * j + 4)
                    dst = (QK[:, 0, t, :], QK[:, 1, t, :], VSG[:, t, :], VATT[:, t, :])[j]
                    dve.tensor_scalar(dst, PS[:, 4 * (j % 2) + t, :], rtok(t), None, ALU.mult)\
                       .then_inc(drained, 1)
                if 0 <= j < 2:
                    dve.wait_ge(qk_sq, 4 * j + t + 1)
                    dve.tensor_reduce(SMALL[:, S_QKS + 8 * (4 * j + t):S_QKS + 8 * (4 * j + t) + 8],
                                      TG1[:].rearrange("p (h d) -> p h d", d=DH), AX.X, ALU.add)\
                       .then_inc(qk_red, 1)
                if n == U_B - 5:
                    dve.wait_ge(qk_red, 8)
                    dve.tensor_scalar(ssq, ssq, 1.0 / DH, EPS, ALU.mult, ALU.add).then_inc(qk_ms, 1)
                if n == U_B - 3:
                    dve.wait_ge(qk_rt, 1)
                    link(dve.reciprocal(ssq, ssq))
                    for i in range(2):
                        for tt in range(TT):
                            c = S_QKS + 8 * (4 * i + tt)
                            v = QK[:, i, tt, :].rearrange("p (h d) -> p h d", d=DH)
                            dve.tensor_tensor(v, v, SMALL[:, c:c + 8].unsqueeze(2)
                                              .broadcast_to([P, HEADS, DH]), ALU.mult)\
                               .then_inc(qk_ready, 1)
                if n == U_B:
                    dve.wait_ge(bc_in, 16 * 12)
                    for tt in range(TT):
                        dve.wait_ge(vg_ready, tt + 1)
                        dve.bn_stats(SMALL[:, S_LN + 6 * tt:S_LN + 6 * tt + 6], VSG[:, tt, :])\
                           .then_inc(vchain, 1)
                        nv += 1
                    dve.wait_ge(vchain, nv)
                    for tt in range(TT):
                        dve.bn_aggr(SMALL[:, S_LN + 24 + 2 * tt:S_LN + 26 + 2 * tt],
                                    SMALL[:, S_LN + 6 * tt:S_LN + 6 * tt + 6]).then_inc(vchain, 1)
                        nv += 1
                    dve.wait_ge(vchain, nv)
                    var = SMALL[:, S_LN + 24:S_LN + 32].rearrange("p (t two) -> p t two", two=2)[:, :, 1]
                    dve.tensor_scalar(SMALL[:, S_LN + 40:S_LN + 44], var, EPS, None, ALU.add)\
                       .then_inc(vg_var, 1)
            dve.wait_ge(vg_sd, 1)
            sd = SMALL[:, S_LN + 40:S_LN + 44]
            link(dve.reciprocal(sd, sd))
            for tt in range(TT):
                link(dve.tensor_scalar(VSG[:, tt, :], VSG[:, tt, :],
                                       SMALL[:, S_LN + 24 + 2 * tt:S_LN + 25 + 2 * tt],
                                       SMALL[:, S_LN + 40 + tt:S_LN + 41 + tt],
                                       ALU.subtract, ALU.mult))
                link(dve.tensor_tensor(VSG[:, tt, :], VSG[:, tt, :], SGLN[:, 0, :], ALU.mult))
                dve.tensor_tensor(VSG[:, tt, :], VSG[:, tt, :], SGLN[:, 1, :], ALU.add)\
                   .then_inc(vn_ready, 1)
            taps_done = 0

            def taps(k):
                nonlocal taps_done
                for _ in range(k):
                    if taps_done == CVK * KW:
                        return
                    pair, rest = divmod(taps_done, 2 * CVK)
                    j, c = rest // 2, 2 * pair + rest % 2
                    if rest == 0:
                        dve.wait_ge(tg_used, 2 * pair + 2)
                    if j == 0:
                        ins = dve.tensor_scalar(CACC[:, c, :], CPAD[:, c, 2:2 + SEQ], col(V_CVW + c),
                                                col(V_CVB + c), ALU.mult, ALU.add)
                    else:
                        dve.wait_ge(c_tap, taps_done - 1)
                        ins = dve.scalar_tensor_tensor(
                            CACC[:, c, :], CPAD[:, c, 2 + j:2 + j + SEQ], col(V_CVW + KW * j + c),
                            CACC[:, c, :], ALU.mult, ALU.add)
                    ins.then_inc(c_tap, 1)
                    taps_done += 1

            tg_jobs = {2: CPAD[:, 0, 32:], 3: CPAD[:, 1, 32:], 6: CPAD[:, 2, 32:],
                       7: CPAD[:, 3, 32:], 8: UU[:, 0, :], 9: UU[:, 1, :], 10: UU[:, 2, :],
                       11: UU[:, 3, :]}
            tg_order = sorted(tg_jobs)

            def tg_mult(i):
                if i in tg_jobs:
                    k = tg_order.index(i)
                    dve.wait_ge(tg_act, k + 1)
                    dve.tensor_tensor(tg_jobs[i], tg_jobs[i], (TG0, TG1)[i % 2][:], ALU.mult)\
                       .then_inc(tg_used, 1)

            for i in range(12):
                dve.wait_ge(unit_done, U_B + i + 1)
                if i in (0, 1, 4, 5):
                    c = i % 4 + (2 if i >= 4 else 0)
                    dst = CPAD[:, c, 32:]
                else:
                    dst = (TG0, TG1)[i % 2][:]
                    if i >= 6:
                        dve.wait_ge(tg_used, tg_order.index(i) - 1)
                dve.tensor_tensor(dst, PS[:, i % 2, :], RBC[:], ALU.mult).then_inc(drained, 1)
                tg_mult(i - 1)
                h = i - 4
                if 0 <= h < HEADS:
                    rows_ = slice(DH * (h % 2), DH * (h % 2) + DH)
                    dve.wait_ge(av_done, h + 1)
                    dve.tensor_copy(ATT[rows_, h // 2, :], PS[rows_, 2 + 3 * (h % 2), :])\
                       .then_inc(att_read, 1)
                h = i - 3
                if 0 <= h < HEADS:
                    b0 = 2 + 3 * (h % 2)
                    dve.wait_ge(tri_done, h + 1)
                    z = PS[:, b0:b0 + 2, 0:P]
                    dve.tensor_tensor(z, z, MMIN[:], ALU.min).then_inc(min_ready, 1)
                    z = PS[:, b0:b0 + 3, :].rearrange("p b c -> p (b c)")[:, 896:1152]
                    dve.tensor_tensor(z, z, MMIN[:].rearrange("p a c -> p (a c)"), ALU.min)\
                       .then_inc(min_ready, 1)
                if i == 0:
                    for q in range(2):
                        dve.wait_ge(wt_t, q + 1)
                        dve.tensor_tensor(WT[:, 4 * q:4 * q + 4, :],
                                          PS[:, 6 + q, :].rearrange("p (g t) -> p g t", t=P),
                                          MINC[:].unsqueeze(1).broadcast_to([P, 4, P]), ALU.mult)\
                           .then_inc(wt_ready, 1)
                lo(U_B + i + 4)
                if i in (1, 2):
                    for c in (2 * i - 2, 2 * i - 1):
                        dve.wait_ge(sg_done, c + 1)
                        dve.tensor_tensor(UU[:, c, :].rearrange("p (n t) -> p n t", t=P),
                                          PS[:, 6 + c % 2, :].rearrange("p (n t) -> p n t", t=P),
                                          SGB[:, c, :].unsqueeze(1).broadcast_to([P, TT, P]), ALU.add)\
                           .then_inc(sg_read, 1)
                h = i - 2
                if 0 <= h < HEADS:
                    b0 = 2 + 3 * (h % 2)
                    dve.wait_ge(ln_ready, h + 1)
                    if h:
                        dve.wait_ge(tri_done, h)
                    dve.scalar_tensor_tensor(
                        SPB[:], PS[:, b0:b0 + 3, :].rearrange("p b c -> p (b c)")[:, 0:1280], 0.0, E1[:],
                        ALU.max, ALU.add).then_inc(sp_ready, 1)
                    dve.wait_ge(sp_ready, 3 * h + 1)
                    z = SPB[:, 0:1024].rearrange("p (a c) -> p a c", a=2)[:, :, 0:P]
                    dve.tensor_tensor(z, z, MSTR[:], ALU.mult).then_inc(sp_ready, 1)
                    z = SPB[:, 896:1152]
                    dve.tensor_tensor(z, z, MSTR[:].rearrange("p a c -> p (a c)"), ALU.mult)\
                       .then_inc(sp_ready, 1)
                if i >= 4:
                    taps(5 if i < 11 else 2)
            tg_mult(11)
            for b in range(3):
                for q in range(2):
                    for r in range(6):
                        n = U_C + 12 * b + 6 * q + r
                        dve.wait_ge(unit_done, n + 1)
                        if r < 4:
                            if b or q:
                                dve.wait_ge(drained, DR_C + 16 * b + 8 * q - 4 + r + 1)
                            dve.tensor_tensor(GS[:, r, :], PS[:, r, :], RBC[:], ALU.mult)\
                               .then_inc(drained, 1)
                        lo(n + 4)
                        if r == 5:
                            for m in range(4):
                                mm = 4 * q + m
                                dve.wait_ge(gs_ready, 8 * b + 4 * q + m + 1)
                                dst = MERG[:, mm, :] if b == 0 else TMPY[:]
                                if b == 2 and mm:
                                    dve.wait_ge(merged, mm)
                                dve.tensor_tensor(dst, PS[:, 4 + m, :], GS[:, m, :], ALU.mult)\
                                   .then_inc(drained, 1)
                                if b:
                                    dve.wait_ge(drained, DR_C + 16 * b + 8 * q + 4 + m + 1)
                                    ins = dve.tensor_tensor(MERG[:, mm, :], MERG[:, mm, :], TMPY[:],
                                                            ALU.add)
                                    if b == 2:
                                        ins.then_inc(merged, 1)
                                    else:
                                        link(ins)
                        if b < 2 and q == 0 and r == 0:
                            src = (UU, ATT)[b]
                            dve.wait_ge(bh_ready, b + 1)
                            dve.tensor_tensor(BL[:], src[:], BH[:].bitcast(F32), ALU.subtract)\
                               .then_inc(bl_ready, 1)
                        taps((5, 5, 5, 5, 8, 0)[r])
                        if b == 1 and q == 1 and r == 1:
                            assert taps_done == CVK * KW
                            dve.wait_ge(c_tap, CVK * KW)
                            link(dve.tensor_tensor(TG1[:], CACC[:, 0, :], CACC[:, 1, :], ALU.add))
                            link(dve.tensor_tensor(TG0[:], CACC[:, 2, :], CACC[:, 3, :], ALU.add))
                            dve.tensor_tensor(TG1[:], TG1[:], TG0[:], ALU.add).then_inc(c_sum, 1)
                        if b == 1 and q == 1 and r == 2:
                            dve.wait_ge(c_mean, 1)
                            for c in range(KW):
                                dve.scalar_tensor_tensor(CACC[:, c, :], PS[:, 4, :], -1.0 / W,
                                                         CACC[:, c, :], ALU.mult, ALU.add)\
                                   .then_inc(c_cent, 1)
                        if b == 1 and q == 1 and r == 3:
                            for c in range(KW):
                                dve.wait_ge(c_sq, c + 1)
                                if c:
                                    dve.wait_ge(c_ssum, c)
                                    ins = dve.tensor_tensor(TG0[:], TG0[:], TG1[:], ALU.add)
                                else:
                                    ins = dve.tensor_copy(TG0[:], TG1[:])
                                ins.then_inc(c_ssum, 1)
                        if b == 2 and q == 0 and r == 0:
                            dve.wait_ge(c_var, 1)
                            dve.tensor_scalar(TG0[:], PS[:, 5, :], 1.0 / W, EPS, ALU.mult, ALU.add)\
                               .then_inc(c_ve, 1)
                            dve.wait_ge(c_sd, 1)
                            link(dve.reciprocal(TG0[:], TG0[:]))
                            for c in range(KW):
                                dve.tensor_tensor(CACC[:, c, :], CACC[:, c, :], TG0[:], ALU.mult)\
                                   .then_inc(c_norm, 1)
                            dve.wait_ge(bh_ready, 3)
                            dve.tensor_tensor(BL[:], CACC[:], BH[:].bitcast(F32), ALU.subtract)\
                               .then_inc(bl_ready, 1)
                    if b == 2:
                        for m in range(4 * q, 4 * q + 4):
                            dve.wait_ge(mh_ready, m + 1)
                            dve.tensor_tensor(ML[:, m, :], MERG[:, m, :], MH[:, m, :].bitcast(F32),
                                              ALU.subtract).then_inc(ml_ready, 1)
            dve.wait_ge(xres_in, 16)
            for m in range(KD):
                dve.wait_ge(unit_done, U_D + m + 1)
                dve.tensor_tensor(X1[:, m, :], PS[:, m % 4, :], X1[:, m, :], ALU.add)\
                   .then_inc(drained, 1)
                dve.wait_ge(drained, DR_D + m + 1)
                feed(1, m, X1, V_LN2)
                lo(U_D + m + 4)
            norm(1)
            dve.wait_ge(r_ready, 4)
            dve.wait_ge(consts, 9)

            def up_conv(r, f0, i):
                c = r % 2 + (NF if r >= 2 else 0) + 2 * f0 + 2 * i
                dve.wait_ge(y_first, 4 * f0 + r + 1 + 4 * i)
                dve.scalar_tensor_tensor(YB[:, r, :], UPB[:, r, 3:515], VEC[:, bass.ds(V_FW[1] + c, 1)],
                                         YB[:, r, :], ALU.mult, ALU.add).then_inc(y_tap, 1)
                dve.wait_ge(y_tap, 4 * f0 + r + 1 + 4 * i)
                dve.scalar_tensor_tensor(YB[:, r, :], UPB[:, r, 2:514], VEC[:, bass.ds(V_FW[0] + c, 1)],
                                         YB[:, r, :], ALU.mult, ALU.add).then_inc(y_conv, 1)

            def up_body(i, f0, last):
                for r in range(4):
                    dve.wait_ge(unit_done, U_E + 4 * f0 + r + 1 + 4 * i)
                    dve.tensor_tensor(UPB[:, r, 4:516], PS[:, r, :], RBC[:], ALU.mult)\
                       .then_inc(drained, 1)
                    if r:
                        up_conv(r - 1, f0, i)
                    if last:
                        lo(U_E + 4 * f0 + r + 4)
                    else:
                        lo(U_E + 4 * f0 + 4 + r, i)
                up_conv(3, f0, i)
                for r in range(2):
                    dve.wait_ge(y_silu, 2 * f0 + r + 1 + 2 * i)
                    if r == 0:
                        dve.wait_ge(y_conv, 4 * f0 + 4 + 4 * i)
                    dve.tensor_tensor(GF[:, bass.ds(2 * f0 + r + 2 * i, 1), :],
                                      YB[:, r:r + 1, :], YB[:, r + 2:r + 3, :], ALU.mult)\
                       .then_inc(gf_ready, 1)

            up_body(0, 0, False)
            with dve.Fori(0, NF // 2 - 2) as i:
                up_body(i, 1, False)

            def ff_lo(kk, i=0):
                dve.wait_ge(fh_ready, kk + 1 + 2 * i)
                dve.tensor_tensor(FL[:, kk % 2], GF[:, bass.ds(2 * kk + 4 * i, 2), :],
                                  FH[:, kk % 2].bitcast(F32), ALU.subtract).then_inc(fl_ready, 1)

            def down_body(kk, i=0, more=True):
                if more:
                    ff_lo(kk + 1, i)
                lo(U_F + 2 * kk + 4, i)
                lo(U_F + 2 * kk + 5, i)

            ff_lo(0)
            up_body(0, NF // 2 - 1, True)
            down_body(0)
            with dve.Fori(0, (NF // 2 - 3) // 2) as i:
                down_body(1, i)
                down_body(2, i)
            down_body(NF // 2 - 2)
            down_body(NF // 2 - 1, more=False)
            for m in range(KD):
                if m % 4 == 0:
                    dve.wait_ge(unit_done, U_G - 1 + m // 4)
                dve.tensor_tensor(X1[:, m, :], PS[:, (m + 4) % 8, :], X1[:, m, :], ALU.add)\
                   .then_inc(drained, 1)
                dve.wait_ge(drained, DR_F + m + 1)
                feed(2, m, X1, V_NG2)
            for j in range(3):
                for t in range(TT):
                    if j == 0:
                        lo(U_G + t + 4)
                    if j == 0 and t == 2:
                        norm(2)
                        dve.wait_ge(r_ready, 6)
                for t in range(TT):
                    if t == 0:
                        dve.wait_ge(unit_done, U_G + 4 * j + 4)
                    if j < 2:
                        dve.tensor_scalar(Q2[:, t, 512 * j:512 * j + 512], PS[:, 4 - 4 * j + t, :], rtok(t),
                                          DH ** -0.5, ALU.mult, ALU.mult).then_inc(drained, 1)
                    else:
                        dve.tensor_scalar(KDUP[:, t, :, 0:DH],
                                          PS[:, 4 + t, 0:256].rearrange("p (g d) -> p g d", d=DH),
                                          rtok(t), None, ALU.mult)
                        dve.tensor_scalar(V2[:, t, :], PS[:, 4 + t, 256:512], rtok(t), None, ALU.mult)\
                           .then_inc(drained, 1)
                    if j == 0:
                        lo(U_G + t + 8)
                    if j == 1:
                        lo(U_G + t + 12)
            dve.wait_ge(drained, DR_G + 12)
            for v, nh in ((Q2[:].rearrange("p t (h d) -> p t h d", d=DH), 16),
                          (KDUP[:], KVH)):
                a, b2 = v[:, :, :, 0:8], v[:, :, :, 8:16]
                cos = ROPE[:, :, 0:8].unsqueeze(2).broadcast_to([P, TT, nh, 8])
                sin = ROPE[:, :, 8:16].unsqueeze(2).broadcast_to([P, TT, nh, 8])
                r_ = [RT[:, z, 0:TT * nh * 8].rearrange("p (t h d) -> p t h d", t=TT, h=nh)
                      for z in range(4)]
                if nh == KVH:
                    dve.wait_ge(rope_ready, 2)
                dve.tensor_tensor(r_[0], a, cos, ALU.mult)
                dve.tensor_tensor(r_[1], b2, sin, ALU.mult)
                dve.tensor_tensor(r_[2], b2, cos, ALU.mult)
                link(dve.tensor_tensor(r_[3], a, sin, ALU.mult))
                dve.tensor_tensor(a, r_[0], r_[1], ALU.subtract).then_inc(rope_ready, 1)
                dve.tensor_tensor(b2, r_[2], r_[3], ALU.add).then_inc(rope_ready, 1)
            dve.wait_ge(rope_ready, 4)
            dve.tensor_copy(KDUP[:, :, :, DH:], KDUP[:, :, :, 0:DH]).then_inc(rope_ready, 1)
            for m in range(KD):
                dve.wait_ge(unit_done, U_GA + m + 1)
                dve.tensor_tensor(YA[:, m, :], PS[:, m % 2, :], RBC[:], ALU.mult).then_inc(drained, 1)
                lo(U_GA + m + 4)

            def window_read(s):
                g, nb = divmod(s, TT)
                dve.wait_ge(pv_done, s + 1)
                ya = YA[:, 2 * g:2 * g + 2, nb * P:(nb + 1) * P]
                dve.tensor_tensor(ya, PS[:, 2, 0:256].rearrange("p (i q) -> p i q", q=P), ya, ALU.mult)\
                   .then_inc(pv_read, 1)

            def att(s, c, n=4):
                return SMALL[:, S_ATT + 20 * (s % 2) + c:S_ATT + 20 * (s % 2) + c + n]

            def window_max(s):
                g, nb = divmod(s, TT)
                buf = S2[s % 2]
                dve.wait_ge(qk2_done, s + 1)
                if s >= 2:
                    dve.wait_ge(pt_t, s - 1)
                mask = AM[:, 1:3, :] if nb else AM[:, 0:3:2, :]
                for par in range(2):
                    dve.tensor_tensor(buf[:, par].rearrange("p i (b c) -> p i b c", b=2),
                                      PS[:, 6 + par, :].rearrange("p (i b c) -> p i b c", i=2, b=2),
                                      mask.unsqueeze(1).broadcast_to([P, 2, 2, P]),
                                      ALU.add).then_inc(s2_mask, 1)
                dve.wait_ge(s2_mask, 2 * s + 2)
                link(dve.tensor_reduce(att(s, 0).rearrange("p (a b) -> p a b", a=2), buf[:], AX.X, ALU.max))
                sink = SINK[:, 4 * g:4 * g + 4].rearrange("p (i a) -> p a i", a=2)
                m2 = att(s, 0).rearrange("p (a b) -> p a b", a=2)
                link(dve.tensor_tensor(m2, m2, sink, ALU.max))
                dve.tensor_scalar(att(s, 4), att(s, 0), -1.0, None, ALU.mult)
                dve.tensor_tensor(att(s, 8).rearrange("p (a b) -> p a b", a=2), sink, m2, ALU.subtract)\
                   .then_inc(s2_max, 1)

            def window_norm(s):
                dve.wait_ge(s2_exp, 5 * s + 5)
                link(dve.tensor_tensor(att(s, 16), att(s, 12), att(s, 8), ALU.add))
                link(dve.reciprocal(att(s, 16), att(s, 16)))
                v = S2[s % 2][:].rearrange("p a b c -> p (a b) c")
                dve.tensor_tensor(v, v, att(s, 16).unsqueeze(2).broadcast_to([P, 4, 256]), ALU.mult)\
                   .then_inc(s2_ready, 1)

            def rec_conv(c):
                dve.wait_ge(uc_first, c + 1)
                for j in (2, 1, 0):
                    ins = dve.scalar_tensor_tensor(
                        UC[c % 2][:], UP2[:, c % 2, 1 + j:1 + j + SEQ], col(V_CW2 + KD * j + c),
                        UC[c % 2][:], ALU.mult, ALU.add)
                    if j:
                        link(ins)
                    else:
                        ins.then_inc(uc_ready, 1)

            def rec_square(c):
                dve.wait_ge(a_sq, c + 1)
                dve.wait_ge(tanh_ready, c + 1)
                dve.scalar_tensor_tensor(RR[c % 2][:], UC[c % 2][:], 1.0, RR[c % 2][:], ALU.add,
                                         ALU.mult).then_inc(bsq_ready, 1)

            def rec_scan(c):
                dve.wait_ge(bsqrt, c + 1)
                dve.wait_ge(iu_ready, c + 1)
                link(dve.tensor_tensor(RR[c % 2][:], RR[c % 2][:], II[c % 2][:], ALU.mult))
                dve.tensor_tensor_scan(YR[:, c, :], YR[:, c, :], RR[c % 2][:], 0.0, ALU.mult, ALU.add)\
                   .then_inc(h_ready, 1)

            dve.wait_ge(consts, 13)
            dve.wait_ge(ya_silu, KD)
            for s in range(19):
                m, q = divmod(s, 4)
                if s < 16:
                    dve.wait_ge(unit_done, U_GR + s + 1)
                    if q < 2:
                        dst = UP2[:, q, 4:516]
                        if m:
                            dve.wait_ge(yg_ready, m)
                    else:
                        dst = GT[:, q - 2, :]
                        if m:
                            dve.wait_ge(yr_ready, 2 * m + q - 3)
                    dve.tensor_tensor(dst, PS[:, s % 2, :], RBC[:], ALU.mult).then_inc(drained, 1)
                if s >= 3:
                    window_read(s - 3)
                if s < 16:
                    lo(U_GR + s + 4)
                if q == 1 and m:
                    rec_square(2 * m - 2)
                    rec_square(2 * m - 1)
                if s < 16:
                    window_max(s)
                if 1 <= s <= 16:
                    window_norm(s - 1)
                if q == 2 and s < 16:
                    rec_conv(2 * m + 1)
                if q == 1 and s < 16:
                    rec_conv(2 * m)
                if q in (1, 2) and m:
                    rec_scan(2 * m + q - 3)
                if s == 18:
                    dve.wait_ge(qk2_done, 16)
                    for k in range(5):
                        dve.wait_ge(bh2_ready, k + 1)
                        dve.tensor_tensor(BL2[:, k, :], YR[:, k, :], BH2[:, k, :].bitcast(F32),
                                          ALU.subtract).then_inc(bl2_ready, 1)
            def low_parts(src, ks, n0):
                for k in ks:
                    dve.wait_ge(bh2_ready, n0 + k + 1)
                    dve.tensor_tensor(BL2[:, k, :], src[:, k, :], BH2[:, k, :].bitcast(F32),
                                      ALU.subtract).then_inc(bl2_ready, 1)

            def merge_body(i0, i=0):
                for r in range(4):
                    n = U_H + 4 * i0 + r
                    dve.wait_ge(unit_done, n + 1 + 4 * i)
                    if r < 2:
                        if i0:
                            dve.wait_ge(drained, DR_H + 4 * i0 + r - 1 + 4 * i)
                        dve.tensor_tensor(GS2[:, r, :], PS[:, r, :], RBC[:], ALU.mult)\
                           .then_inc(drained, 1)
                    else:
                        m = 2 * (i0 % 4) + r - 2
                        tile = MERG2[:, bass.ds(m + 2 * i, 1), :]
                        if i0 >= 4 and m:
                            dve.wait_ge(merged2, m + 2 * i)
                        dve.wait_ge(gs2_ready, 2 * i0 + r - 1 + 2 * i)
                        dst = tile if i0 < 4 else TMP2[:].unsqueeze(1)
                        dve.tensor_tensor(dst, PS[:, r:r + 1, :], GS2[:, r - 2:r - 1, :], ALU.mult)\
                           .then_inc(drained, 1)
                        if i0 >= 4:
                            dve.wait_ge(drained, DR_H + 4 * i0 + r + 1 + 4 * i)
                            dve.tensor_tensor(tile, tile, TMP2[:].unsqueeze(1), ALU.add)\
                               .then_inc(merged2, 1)
                    lo(n + 4, i)
                if i0 >= 4:
                    for m in (2 * i0 - 8, 2 * i0 - 7):
                        dve.wait_ge(m2h_ready, m + 1 + 2 * i)
                        dve.tensor_tensor(M2L[:, bass.ds(m + 2 * i, 1), :],
                                          MERG2[:, bass.ds(m + 2 * i, 1), :],
                                          M2H[:, bass.ds(m + 2 * i, 1), :].bitcast(F32),
                                          ALU.subtract).then_inc(m2l_ready, 1)

            low_parts(YR, range(5, KD), 0)
            merge_body(0)
            with dve.Fori(0, 3) as i:
                merge_body(1, i)
            dve.wait_ge(pv_read, 16)
            low_parts(YA, range(KD), KD)
            merge_body(4)
            with dve.Fori(0, 2) as i:
                merge_body(5, i)
            merge_body(7)
            for i in range(4):
                lo(U_O + i + 4)
            for c in range(2):
                dve.wait_ge(unit_done, U_O + 4 * c + 4)
                for t in range(TT):
                    dve.wait_ge(x2t_ready, t + 1)
                    v = XT2[:, t, c * 512:c * 512 + 512]
                    dve.tensor_tensor(v, PS[:, 4 * c + t, :], v, ALU.add).then_inc(drained, 1)
            dve.wait_ge(fg_in, 16)
            for t in range(TT):
                s_ = SMALL[:, S_FIN + t:S_FIN + t + 1]
                dve.wait_ge(fin_sq, t + 1)
                dve.tensor_scalar(s_, s_, 1.0 / D, EPS, ALU.mult, ALU.add).then_inc(fin_ms, 1)
            for t in range(TT):
                s_ = SMALL[:, S_FIN + t:S_FIN + t + 1]
                dve.wait_ge(fin_sd, t + 1)
                link(dve.reciprocal(s_, s_))
                dve.scalar_tensor_tensor(XT2[:, t, :], XT2[:, t, :], s_, FG[:], ALU.mult, ALU.mult)\
                   .then_inc(fin_ready, 1)

        @block.tensor
        def _(pe):
            def mm(out_, lhsT, rhs, start, stop):
                return pe.matmul(out_, lhsT, rhs, start=start, stop=stop, skip_group_check=True)

            def split_mm(out_, lh, ll, rh, rl, start, stop):
                mm(out_, lh, rh, start, False)
                mm(out_, lh, rl, False, False)
                return mm(out_, ll, rh, False, stop)

            def unit(n, i=0):
                pe.wait_ge(hi_done, n + 1 + i)
                pe.wait_ge(lo_done, n + 1 + i)

            def cm_unit(n, bank, mh, ml, i=0, ready=None):
                unit(n, i)
                wh, wl = ring(WH, n), ring(WL, n)
                for k in range(KD):
                    if ready:
                        ready(k)
                    last = split_mm(PS[:, bank, :], wh[:, k, :], wl[:, k, :], mh[:, k, :], ml[:, k, :],
                                    k == 0, k == KD - 1)
                last.then_inc(unit_done, 1)

            def quad_unit(n, half, bank0, mh, ml, nk, i=0):
                unit(n, i)
                wh, wl = ring(WH, n), ring(WL, n)
                for m in range(4):
                    for k in range(2):
                        kk = 2 * half + k
                        last = split_mm(PS[:, bank0 + m, :], wh[:, k, m * P:(m + 1) * P],
                                        wl[:, k, m * P:(m + 1) * P], mh[:, kk, :], ml[:, kk, :],
                                        kk == 0, kk == nk - 1)
                last.then_inc(unit_done, 1)

            def tm_unit(n, u, bank0, xh, xl, ready=None, free=None):
                unit(n)
                wh, wl = ring(WH, n), ring(WL, n)
                for t in range(TT):
                    if u == 0 and free:
                        free(t)
                    for k in range(2):
                        kk = 2 * u + k
                        if ready and t == 0:
                            ready(kk)
                        ts = slice(t * P, (t + 1) * P)
                        last = split_mm(PS[:, bank0 + t, :], xh[:, kk, ts], xl[:, kk, ts],
                                        wh[:, k, :], wl[:, k, :], kk == 0, kk == KD - 1)
                last.then_inc(unit_done, 1)

            def x_parts(e):
                def ready(k):
                    pe.wait_ge(xh_ready, KD * e + k + 1)
                    pe.wait_ge(xl_ready, KD * e + k + 1)
                return ready

            def stats(e):
                pe.wait_ge(ss_added, KD * (e + 1))
                b = 2 if e == 2 else 6
                mm(PS[:, b + 1, :], ONES[:], SS[:], True, True)
                for t in range(TT):
                    last = mm(PS[:, b, t:t + 1], SS[:, t * P:(t + 1) * P], ONES[:, 0:1], True, True)
                last.then_inc(stat_done, 1)

            def tr(out_, in_):
                return pe.transpose(out_, in_, IDENT[:])

            pe.wait_ge(consts, 2)
            for t in range(TT):
                pe.wait_ge(x_in[t], 16)
                for k in range(KD):
                    last = tr(PS[:, k, t * P:(t + 1) * P], XTOK[:, t, k * P:(k + 1) * P])
                    if t == TT - 1:
                        last.then_inc(xt_done, 1)
            pe.wait_ge(vec_in, 16 * N_VEC)
            pe.wait_ge(drained, 1)
            for r in range(4):
                last = tr(PS[:, 0, r * P:(r + 1) * P], ROWS[:, r, :])
            last.then_inc(vec_t, 1)
            pe.wait_ge(vec_ready, 2)
            for j in range(4):
                for u in range(4):
                    n = U_A + 4 * j + u
                    tm_unit(n, u, 4 * (j % 2), XH, XL, x_parts(0) if j == 0 else None,
                            lambda t: pe.wait_ge(drained, 4 * j + t + 1))
                    if n == 2:
                        pe.wait_ge(drained, KD)
                        stats(0)
                    if n == 3:
                        pe.wait_ge(ms_ready, 2)
            packed = [(0, 0, 512), (512, 1, 384), (1024, 2, 256), (896, 3, 128)]

            def head_z(h, c0, n):
                b0 = 2 + 3 * (h % 2)
                return PS[:, b0 + c0 // 512, c0 % 512:c0 % 512 + n]

            for i in range(12):
                pe.wait_ge(drained, DR_B + i - 1 if i >= 2 else DR_A + 8 + i + 1)
                cm_unit(U_B + i, i % 2, XH, XL)
                if i == 0:
                    pe.wait_ge(drained, DR_B)
                if i < 2:
                    pe.wait_ge(qk_ready, 4 * i + 4)
                    for c in range(KW):
                        if i:
                            pe.wait_ge(qkt_ready, c + 1)
                        for t in range(TT):
                            last = tr(PS[:, 2 + c, t * P:(t + 1) * P], QK[:, i, t, c * P:(c + 1) * P])
                        last.then_inc(qkt_t, 1)
                if i == 0:
                    pe.wait_ge(sgw_in, 16)
                    for q in range(2):
                        for g in range(4):
                            last = tr(PS[:, 6 + q, g * P:(g + 1) * P], SGW[:, 4 * q + g, :])
                        last.then_inc(wt_t, 1)
                h = i - 4
                if 0 <= h < HEADS:
                    pe.wait_ge(a_ready, h + 1)
                    rows_ = slice(DH * (h % 2), DH * (h % 2) + DH)
                    for c0, j, w in packed:
                        last = mm(PS[rows_, 2 + 3 * (h % 2), SEQ - w:SEQ], VATT[:, j, h * DH:(h + 1) * DH],
                                  ABUF[:, c0:c0 + w], j == 0, j == 3)
                    last.then_inc(av_done, 1)
                h = i - 3
                if 0 <= h < HEADS:
                    pe.wait_ge(sp_ready, 3 * h + 3)
                    for c0, j, w in packed:
                        last = mm(head_z(h, c0, w), NTRI[:], SPB[:, c0:c0 + w], False, False)
                        for c1, j1, w1 in packed:
                            if j1 > j:
                                last = mm(head_z(h, c0 + w - w1, w1), NONE_[:], SPB[:, c1:c1 + w1],
                                          False, False)
                    last.then_inc(tri_done, 1)
                h = i - 2
                if 0 <= h < HEADS:
                    if h == 0:
                        pe.wait_ge(qkt_ready, 8)
                        pe.wait_ge(consts, 8)
                    elif h == 1:
                        pe.wait_ge(sg_read, 4)
                    else:
                        pe.wait_ge(att_read, h - 1)
                    rows_ = slice(DH * (h % 2), DH * (h % 2) + DH)
                    for c0, j, w in packed:
                        last = mm(head_z(h, c0, w), QKT[rows_, 1, h // 2, j * P:(j + 1) * P],
                                  QKT[rows_, 0, h // 2, SEQ - w:SEQ], j != 3, False)
                    last.then_inc(sc_done, 1)
                if i in (1, 2):
                    if i == 1:
                        pe.wait_ge(wt_ready, 2)
                        pe.wait_ge(vn_ready, TT)
                    for c in (2 * i - 2, 2 * i - 1):
                        if i == 2:
                            pe.wait_ge(sg_read, c - 1)
                        for g in (2 * c, 2 * c + 1):
                            for t in range(TT):
                                last = mm(PS[g % 2 * DH:(g % 2 + 1) * DH, 6 + c % 2, t * P:(t + 1) * P],
                                          VSG[:, t, g * DH:(g + 1) * DH], WT[:, g, :], True, True)
                        last.then_inc(sg_done, 1)

            def branch(b, i, ln):
                n0 = U_C + 12 * b
                for q in range(2):
                    for r in range(4):
                        if b == 0 and q == 0:
                            pe.wait_ge(drained, DR_C)
                        else:
                            pe.wait_ge(drained, DR_C + 16 * b + 8 * q - 8 + r + 1 + 16 * i)
                        cm_unit(n0 + 6 * q + r, r, XH, XL, 12 * i)
                        if ln == 1 and q == 1 and r == 2:
                            pe.wait_ge(c_sum, 1)
                            pe.wait_ge(drained, DR_C + 24)
                            mm(PS[:, 4, :], ONES[:], TG1[:], True, True).then_inc(c_mean, 1)
                        if ln == 1 and q == 1 and r == 3:
                            pe.wait_ge(c_cent, KW)
                        if ln == 2 and q == 0 and r == 0:
                            pe.wait_ge(c_ssum, KW)
                            pe.wait_ge(drained, DR_C + 32)
                            mm(PS[:, 5, :], ONES[:], TG0[:], True, True).then_inc(c_var, 1)
                    if q == 0:
                        pe.wait_ge(bh_ready, b + 1 + i)
                        pe.wait_ge(bl_ready, b + 1 + i)
                    if ln == 2 and q == 0:
                        pe.wait_ge(c_ve, 1)
                    pe.wait_ge(drained, DR_C + 16 * b + 8 * q + 16 * i)
                    for u in range(2):
                        quad_unit(n0 + 6 * q + 4 + u, u, 4, BH, BL, KW, 12 * i)

            pe.wait_ge(att_read, HEADS)
            branch(0, 0, 0)
            branch(1, 0, 1)
            branch(2, 0, 2)

            for m in range(KD):
                pe.wait_ge(drained, DR_D - 7 + m if m < 4 else DR_D + m - 3)

                def ready(k):
                    pe.wait_ge(mh_ready, k + 1)
                    pe.wait_ge(ml_ready, k + 1)
                cm_unit(U_D + m, m % 4, MH, ML, 0, ready if m == 0 else None)

            def up_body(f0, i, first):
                for r in range(4):
                    pe.wait_ge(drained, DR_E + 4 * f0 - 4 + r + 1 + 4 * i)
                    cm_unit(U_E + 4 * f0 + r, r, XH, XL, 4 * i, x_parts(1) if first and r == 0 else None)
                    if first and r == 0:
                        stats(1)

            up_body(0, 0, True)
            with pe.Fori(0, NF // 2 - 1) as i:
                up_body(1, i, False)

            def down_body(kk, i, start, stop):
                pe.wait_ge(fh_ready, kk + 1 + i)
                pe.wait_ge(fl_ready, kk + 1 + i)
                for half in range(2):
                    n = U_F + 2 * kk + half
                    if start and half == 0:
                        pe.wait_ge(ms_ready, 4)
                    elif start:
                        pe.wait_ge(drained, DR_F)
                    unit(n, 2 * i)
                    wh, wl = ring(WH, n), ring(WL, n)
                    for m in range(4):
                        for k in range(2):
                            last = split_mm(PS[:, 4 - 4 * half + m, :], wh[:, k, m * P:(m + 1) * P],
                                            wl[:, k, m * P:(m + 1) * P], FH[:, kk % 2, k, :],
                                            FL[:, kk % 2, k, :], start and k == 0, stop and k == 1)
                    last.then_inc(unit_done, 1)

            down_body(0, 0, True, False)
            with pe.Fori(0, (NF // 2 - 3) // 2) as i:
                down_body(1, 2 * i, False, False)
                down_body(2, 2 * i, False, False)
            down_body(NF // 2 - 2, 0, False, False)
            down_body(NF // 2 - 1, 0, False, True)

            for j in range(3):
                for u in range(4):
                    n = U_G + 4 * j + u
                    if j == 1 and u == 0:
                        pe.wait_ge(ms_ready, 6)
                    tm_unit(n, u, 4 - 4 * (j % 2), XH, XL, x_parts(2) if j == 0 else None,
                            lambda t: pe.wait_ge(drained, (DR_F, DR_F + 4, DR_G)[j] + t + 1))
                    if j == 0 and u == 2:
                        pe.wait_ge(drained, DR_G)
                        stats(2)
            for i in range(KD + 1):
                if i < KD:
                    pe.wait_ge(drained, DR_GA - 1 + i if i >= 2 else DR_G + 8)
                    cm_unit(U_GA + i, i % 2, XH, XL)
                if i == 0:
                    continue
                m = i - 1
                if m == 0:
                    pe.wait_ge(rope_ready, 5)
                if m >= 2:
                    pe.wait_ge(q2t_ready, (m - 1) + max(0, m - 2 - 4))
                for t in range(TT):
                    last = tr(PS[:, 4 + m % 2, t * P:(t + 1) * P], Q2[:, t, m * P:(m + 1) * P])
                last.then_inc(rt_t, 1)
                if m >= 4:
                    if m >= 6:
                        pe.wait_ge(q2t_ready, 2 * (m - 2) - 2)
                    for t in range(TT):
                        last = tr(PS[:, 6 + m % 2, t * P:(t + 1) * P], KDUP[:, t, m - 4, :])
                    last.then_inc(rt_t, 1)
            def block_diagonal(c):
                pe.wait_ge(uc_ready, c + 1)
                if c:
                    pe.wait_ge(gate_ri, 2 * c)
                else:
                    pe.wait_ge(lruw_in, 32)
                mm(PS[:, 2, :], LRUW[:, c, :], UC[c % 2][:], True, True)
                mm(PS[:, 3, :], LRUW[:, KD + c, :], UC[c % 2][:], True, True).then_inc(bd_done, 1)

            for s in range(19):
                if s < 16:
                    pe.wait_ge(drained, DR_GR + s - 1)
                    cm_unit(U_GR + s, s % 2, XH, XL)
                elif s < 18:
                    pe.wait_ge(drained, DR_GR + s - 1)
                    cm_unit(U_H + s - 16, s % 2, XH, XL)
                if s >= 3:
                    g, nb = divmod(s - 3, TT)
                    pe.wait_ge(pt_ready, s - 2)
                    if s >= 4:
                        pe.wait_ge(pv_read, s - 3)
                        pe.wait_ge(gate_ri, 2 * (s // 4) + 2 * ((s - 1) // 4))
                    kbs = (0, 1) if nb else (1,)
                    for par in range(2):
                        for kb in kbs:
                            last = mm(PS[par * DH:(par + 1) * DH, 2, 0:256],
                                      V2[:, nb - 1 + kb, g * DH:(g + 1) * DH],
                                      PT[:, kb, par].rearrange("p i q -> p (i q)"),
                                      kb == kbs[0], kb == 1)
                    last.then_inc(pv_done, 1)
                if 2 <= s < 18:
                    pe.wait_ge(s2_ready, s - 1)
                    if s >= 3:
                        pe.wait_ge(pt_ready, s - 2)
                    else:
                        pe.wait_ge(q2t_ready, KD + KVH)
                    for kb in range(2):
                        for par in range(2):
                            for idx in range(2):
                                c = (2 * par + idx) * P
                                last = tr(PS[:, 4 + kb, c:c + P],
                                          S2[s % 2][:, par, idx, kb * P:(kb + 1) * P])
                    last.then_inc(pt_t, 1)
                if s < 16:
                    g, nb = divmod(s, TT)
                    if s == 0:
                        pe.wait_ge(q2t_ready, KD + KVH)
                        pe.wait_ge(consts, 13)
                    if s >= 1:
                        pe.wait_ge(s2_mask, 2 * s)
                    for par in range(2):
                        rows_ = slice(par * DH, (par + 1) * DH)
                        for idx in range(2):
                            last = mm(PS[:, 6 + par, idx * 256:idx * 256 + 256],
                                      Q2T[rows_, 2 * g + idx, nb * P:(nb + 1) * P],
                                      K2T[rows_, g, nb * P:nb * P + 256], True, True)
                    last.then_inc(qk2_done, 1)
                if s % 4 == 3 or s and s % 4 == 0:
                    pe.wait_ge(pv_read, s - 2)
                    block_diagonal(s // 2 - 1)
            def merge_body(i0, i):
                for r in range(2 if i0 == 0 else 0, 4):
                    if i0 == 0:
                        pe.wait_ge(gate_ri, 2 * KD)
                    else:
                        pe.wait_ge(drained, DR_H + 4 * i0 - 4 + r + 1 + 4 * i)
                    n = U_H + 4 * i0 + r
                    if r < 2:
                        cm_unit(n, r, XH, XL, 4 * i)
                    else:
                        def ready(k):
                            pe.wait_ge(bh2_ready, 2 * i0 + k + 1)
                            pe.wait_ge(bl2_ready, 2 * i0 + k + 1)
                        cm_unit(n, r, BH2, BL2, 4 * i, ready if i0 in (0, 4) and r == 2 else None)

            merge_body(0, 0)
            with pe.Fori(0, 3) as i:
                merge_body(1, i)
            merge_body(4, 0)
            with pe.Fori(0, 3) as i:
                merge_body(5, i)
            pe.wait_ge(pv_read, 16)
            for t in range(TT):
                if t >= 2:
                    pe.wait_ge(x2t_ready, t - 1)
                for k in range(KD):
                    last = tr(PS[:, 4 + 2 * (t % 2) + k // 4, k % 4 * P:(k % 4 + 1) * P],
                              X1[:, k, t * P:(t + 1) * P])
                last.then_inc(x2t_t, 1)

            def m2_parts(k):
                pe.wait_ge(m2h_ready, k + 1)
                pe.wait_ge(m2l_ready, k + 1)

            for c in range(2):
                for u in range(4):
                    tm_unit(U_O + 4 * c + u, u, 4 * c, M2H, M2L, m2_parts if c == 0 else None,
                            lambda t: pe.wait_ge(drained, DR_O) if c == 0
                            else pe.wait_ge(x2t_ready, TT))


INPUTS = ["x", "ln1_g", "w_in", "b_gate", "sg_ln_g", "sg_ln_b", "sg_w", "sg_b", "w_a_out", "cv_w",
          "cv_b", "cv_ln_g", "cv_ln_b", "w_b_out", "q_norm_g", "k_norm_g", "w_c_out", "w_out", "ln2_g",
          "w_up", "ffn_conv_w", "ffn_conv_b", "w_down", "norm_g_2", "w_in_2", "conv_w_2", "conv_b_2",
          "lru_w_a_2", "lru_b_a_2", "lru_w_x_2", "lru_b_x_2", "lru_lambda_2", "attn_sinks_2",
          "w_rnn_out_2", "w_attn_out_2", "w_o_2", "final_norm_g_2"]


def rope_table():
    import numpy as np
    pos = np.arange(SEQ, dtype=np.float32)
    freq = np.float32(ROPE_THETA) ** (-np.arange(0, ROPE_DIM, 2, dtype=np.float32)
                                      / np.float32(ROPE_DIM))
    ang = (pos[:, None] * freq[None, :]).astype(np.float32)
    return np.concatenate([np.cos(ang), np.sin(ang)], axis=1).astype(np.float32)


def kernel(**inputs):
    import numpy as np
    import concourse.bacc as bacc
    from concourse.bass_utils import run_bass_kernel_spmd

    nc = bacc.Bacc("TRN2", target_bir_lowering=False, num_devices=1)
    arrays = {f"in_{name}": np.ascontiguousarray(inputs[name]) for name in INPUTS}
    arrays["in_rope"] = rope_table()
    args = [nc.dram_tensor(name, a.shape, mybir.dt.from_np(a.dtype), kind="ExternalInput").ap()
            for name, a in arrays.items()]
    out = nc.dram_tensor("out", inputs["x"].shape, F32, kind="ExternalOutput").ap()
    program(nc, *args, out)
    result = run_bass_kernel_spmd(nc, [arrays], core_ids=[0])
    return result.results[0]["out"]
```
